# Optimizing a Trainium2 kernel written in Bass

```python
import math
import jax, jax.numpy as jnp
from jax import lax
import numpy as np

D_MODEL = 1024
BATCH = 1
SEQ = 256
DEPTH = 1

D_MIX = D_MODEL
C_CONV = D_MIX // 4
C_POOL = D_MIX // 4
C_ATTN = D_MIX - C_CONV - C_POOL
DIFF_HEADS = 4
DIFF_HEAD_DIM = C_ATTN // (2 * DIFF_HEADS)
CONV_WIDTH = 31
POOL_WINDOWS = (2, 4, 8, 16)
POOL_GROUP = C_POOL // len(POOL_WINDOWS)
N_IN = 2 * C_CONV + C_POOL + 3 * C_ATTN
N_EXPERT_GROUPS = 4
EXPERTS_PER_GROUP = 4
N_EXPERTS = N_EXPERT_GROUPS * EXPERTS_PER_GROUP
D_EXPERT = D_MODEL // 4
MOE_TOP_K = 2
ATTN_BLOCK = 128
NORM_EPS = 1e-6


def rms_norm(x, g):
    xf = x.astype(jnp.float32)
    y = xf * lax.rsqrt(jnp.mean(xf * xf, axis=-1, keepdims=True) + NORM_EPS)
    return (y * g.astype(jnp.float32)).astype(x.dtype)

def layer_norm(x, g, b):
    xf = x.astype(jnp.float32)
    mu = jnp.mean(xf, axis=-1, keepdims=True)
    xc = xf - mu
    y = xc * lax.rsqrt(jnp.mean(xc * xc, axis=-1, keepdims=True) + NORM_EPS)
    return (y * g.astype(jnp.float32) + b.astype(jnp.float32)).astype(x.dtype)

def alibi_slopes(n_heads):
    start = 2.0 ** (-8.0 / n_heads)
    return jnp.asarray(np.array([start ** (i + 1) for i in range(n_heads)], dtype=np.float32))

def conv_mixer(a_val, a_gate, w_dw, b_dw, ln_g, ln_b, w_pw, b_pw):
    u = a_val * jax.nn.sigmoid(a_gate)
    y = lax.conv_general_dilated(
        u, w_dw[:, None, :].astype(u.dtype), window_strides=(1,),
        padding=[(CONV_WIDTH - 1, 0)],
        dimension_numbers=("NWC", "WIO", "NWC"),
        feature_group_count=C_CONV) + b_dw
    y = jax.nn.silu(layer_norm(y, ln_g, ln_b))
    return y @ w_pw + b_pw

def pool_mixer(u, w_pool, scale):
    s_len = u.shape[1]
    uf = u.astype(jnp.float32)
    c0 = jnp.pad(lax.cumsum(uf, axis=1), ((0, 0), (1, 0), (0, 0)))
    t = jnp.arange(s_len)
    outs = []
    for gi, win in enumerate(POOL_WINDOWS):
        sl = slice(gi * POOL_GROUP, (gi + 1) * POOL_GROUP)
        lo = jnp.maximum(t + 1 - win, 0)
        window_sum = c0[:, 1:, sl] - c0[:, lo, sl]
        count = jnp.minimum(t + 1, win).astype(jnp.float32)[None, :, None]
        d = (window_sum / count - uf[:, :, sl]).astype(u.dtype)
        outs.append(jnp.einsum("bsc,cd->bsd", d, w_pool[gi]))
    return jnp.concatenate(outs, axis=-1) * scale

def diff_attention(q, k, v, lam, slopes):
    s_len = q.shape[1]
    q = q.transpose(0, 2, 3, 1, 4)
    k = k.transpose(0, 2, 3, 1, 4)
    v = v.transpose(0, 2, 1, 3)
    scale = DIFF_HEAD_DIM ** -0.5
    outs = []
    for blk in range(s_len // ATTN_BLOCK):
        q0 = blk * ATTN_BLOCK
        end = q0 + ATTN_BLOCK
        qb = q[:, :, :, q0:end]
        kb = k[:, :, :, :end]
        vb = v[:, :, :end]
        s = jnp.einsum("bhmqd,bhmkd->bhmqk", qb, kb,
                       preferred_element_type=jnp.float32) * scale
        tq = jnp.arange(q0, end)[:, None]
        tk = jnp.arange(end)[None, :]
        dist = (tq - tk).astype(jnp.float32)
        s = s - slopes[None, :, None, None, None] * dist
        s = jnp.where(tk <= tq, s, -jnp.inf)
        p = jax.nn.softmax(s, axis=-1)
        a = p[:, :, 0] - lam * p[:, :, 1]
        outs.append(jnp.einsum("bhqk,bhkd->bhqd", a.astype(vb.dtype), vb))
    o = jnp.concatenate(outs, axis=2)
    return o.transpose(0, 2, 1, 3)

def hier_moe(h, wg, bg, we, be, w_gate, w_up, w_down):
    b_, s_, d_ = h.shape
    t = h.reshape(-1, d_)
    pg = jax.nn.softmax((t @ wg).astype(jnp.float32) + bg.astype(jnp.float32), axis=-1)
    g_idx = jnp.argmax(pg, axis=-1)
    g_p = jnp.take_along_axis(pg, g_idx[:, None], axis=1)[:, 0]
    le = ((t @ we).astype(jnp.float32) + be.astype(jnp.float32)).reshape(-1, N_EXPERT_GROUPS, EXPERTS_PER_GROUP)
    le = jnp.take_along_axis(le, g_idx[:, None, None], axis=1)[:, 0]
    pe = jax.nn.softmax(le, axis=-1)
    top_p, top_i = lax.top_k(pe, MOE_TOP_K)
    top_p = top_p / jnp.sum(top_p, axis=-1, keepdims=True)
    weights = g_p[:, None] * top_p
    eid = g_idx[:, None] * EXPERTS_PER_GROUP + top_i
    gates = jnp.sum(jax.nn.one_hot(eid, N_EXPERTS, dtype=jnp.float32) * weights[..., None], axis=1)
    gates = gates.astype(t.dtype)
    y = jnp.zeros_like(t)
    for e in range(N_EXPERTS):
        act = jax.nn.silu(t @ w_gate[e]) * (t @ w_up[e]) * gates[:, e:e + 1]
        y = y + act @ w_down[e]
    return y.reshape(b_, s_, d_)

def first_inputs(seed: int = 0) -> dict:
    key = jax.random.key(seed)
    ks = iter(jax.random.split(key, 40))
    L = DEPTH

    def nrm(shape, scale):
        return jax.random.normal(next(ks), shape, jnp.float32) * scale

    def gain(shape):
        return 1.0 + nrm(shape, 0.02)

    return {
        "x": nrm((BATCH, SEQ, D_MODEL), 1.0),
        "attn_norm_g": gain((L, D_MODEL)),
        "w_in": nrm((L, D_MODEL, N_IN), D_MODEL ** -0.5),
        "conv_w": nrm((L, CONV_WIDTH, C_CONV), CONV_WIDTH ** -0.5),
        "conv_b": nrm((L, C_CONV), 0.02),
        "conv_ln_g": gain((L, C_CONV)),
        "conv_ln_b": nrm((L, C_CONV), 0.02),
        "conv_pw_w": nrm((L, C_CONV, C_CONV), C_CONV ** -0.5),
        "conv_pw_b": nrm((L, C_CONV), 0.02),
        "pool_w": nrm((L, len(POOL_WINDOWS), POOL_GROUP, POOL_GROUP), POOL_GROUP ** -0.5),
        "pool_scale": gain((L, C_POOL)),
        "q_norm_g": gain((L, DIFF_HEAD_DIM)),
        "k_norm_g": gain((L, DIFF_HEAD_DIM)),
        "lambda_q1": nrm((L, DIFF_HEAD_DIM), 0.1),
        "lambda_k1": nrm((L, DIFF_HEAD_DIM), 0.1),
        "lambda_q2": nrm((L, DIFF_HEAD_DIM), 0.1),
        "lambda_k2": nrm((L, DIFF_HEAD_DIM), 0.1),
        "attn_sub_norm_g": gain((L, 2 * DIFF_HEAD_DIM)),
        "w_out": nrm((L, D_MIX, D_MODEL), D_MIX ** -0.5),
        "ffn_norm_g": gain((L, D_MODEL)),
        "router_g_w": nrm((L, D_MODEL, N_EXPERT_GROUPS), D_MODEL ** -0.5),
        "router_g_b": nrm((L, N_EXPERT_GROUPS), 0.01),
        "router_e_w": nrm((L, D_MODEL, N_EXPERTS), D_MODEL ** -0.5),
        "router_e_b": nrm((L, N_EXPERTS), 0.01),
        "w_gate": nrm((L, N_EXPERTS, D_MODEL, D_EXPERT), D_MODEL ** -0.5),
        "w_up": nrm((L, N_EXPERTS, D_MODEL, D_EXPERT), D_MODEL ** -0.5),
        "w_down": nrm((L, N_EXPERTS, D_EXPERT, D_MODEL), D_EXPERT ** -0.5),
    }

def first_block(x, attn_norm_g, w_in, conv_w, conv_b, conv_ln_g, conv_ln_b, conv_pw_w, conv_pw_b,
              pool_w, pool_scale, q_norm_g, k_norm_g, lambda_q1, lambda_k1, lambda_q2, lambda_k2,
              attn_sub_norm_g, w_out, ffn_norm_g, router_g_w, router_g_b, router_e_w, router_e_b,
              w_gate, w_up, w_down):
    b_, s_, _ = x.shape
    slopes = alibi_slopes(DIFF_HEADS)
    splits = [C_CONV, 2 * C_CONV, 2 * C_CONV + C_POOL,
              2 * C_CONV + C_POOL + C_ATTN, 2 * C_CONV + C_POOL + 2 * C_ATTN]
    for l in range(DEPTH):
        h = rms_norm(x, attn_norm_g[l])
        z = h @ w_in[l]
        a_val, a_gate, p_in, q, k, v = jnp.split(z, splits, axis=-1)

        y_conv = conv_mixer(a_val, a_gate, conv_w[l], conv_b[l], conv_ln_g[l], conv_ln_b[l],
                            conv_pw_w[l], conv_pw_b[l])
        y_pool = pool_mixer(p_in, pool_w[l], pool_scale[l])

        q = rms_norm(q.reshape(b_, s_, DIFF_HEADS, 2, DIFF_HEAD_DIM), q_norm_g[l])
        k = rms_norm(k.reshape(b_, s_, DIFF_HEADS, 2, DIFF_HEAD_DIM), k_norm_g[l])
        v = v.reshape(b_, s_, DIFF_HEADS, 2 * DIFF_HEAD_DIM)
        lam_init = 0.8 - 0.6 * math.exp(-0.3 * l)
        lam = (jnp.exp(jnp.sum(lambda_q1[l].astype(jnp.float32) * lambda_k1[l].astype(jnp.float32)))
               - jnp.exp(jnp.sum(lambda_q2[l].astype(jnp.float32) * lambda_k2[l].astype(jnp.float32)))
               + lam_init)
        o = diff_attention(q, k, v, lam, slopes)
        o = rms_norm(o, attn_sub_norm_g[l]) * (1.0 - lam_init)
        y_attn = o.reshape(b_, s_, C_ATTN)

        mix = jnp.concatenate([y_conv, y_pool, y_attn], axis=-1)
        x = x + mix @ w_out[l]

        hf = rms_norm(x, ffn_norm_g[l])
        x = x + hier_moe(hf, router_g_w[l], router_g_b[l], router_e_w[l], router_e_b[l],
                         w_gate[l], w_up[l], w_down[l])
    return x


DEPTH_2 = 2

HEAD_DIM = 64
A_Q_HEADS = 8
A_KV_HEADS = 2
WINDOW = 128
B_HEADS = 8
WIN_ROWS = 8
WIN_COLS = 16
QCOLS = 16
KCOLS = QCOLS + WIN_COLS
C_Q_HEADS = 8
C_KV_HEADS = 2

A_Q = A_Q_HEADS * HEAD_DIM
A_KV = A_KV_HEADS * HEAD_DIM
B_W = B_HEADS * HEAD_DIM
C_Q = C_Q_HEADS * HEAD_DIM
C_KV = C_KV_HEADS * HEAD_DIM
BRANCH_WIDTH = A_Q
N_BRANCH = 3
IN_SIZES = (A_Q, A_KV, A_KV, B_W, B_W, B_W, C_Q, C_KV, C_KV, N_BRANCH * D_MODEL)
N_IN_2 = A_Q + 2 * A_KV + 3 * B_W + C_Q + 2 * C_KV + N_BRANCH * D_MODEL

D_FF = 2816
META = 16
BLOCK = 128
PAD_FRONT = BLOCK - META
GRID_W = 64
ROPE_THETA = 10000.0
EPS = 1e-6
NEG = -1e30


def rms_norm_2(x, g):
    xf = x.astype(jnp.float32)
    y = xf * lax.rsqrt(jnp.mean(xf * xf, axis=-1, keepdims=True) + EPS)
    return (y * g.astype(jnp.float32)).astype(x.dtype)

def swiglu(h, w_in, w_out):
    gate, up = jnp.split(h @ w_in, 2, axis=-1)
    return (jax.nn.silu(gate) * up) @ w_out

def rope_angles(pos, dim):
    inv_freq = ROPE_THETA ** (-jnp.arange(0, dim, 2, dtype=jnp.float32) / dim)
    return pos.astype(jnp.float32)[:, None] * inv_freq[None, :]

def apply_rope(x, ang):
    half = x.shape[-1] // 2
    cos = jnp.cos(ang)[None, :, None, :]
    sin = jnp.sin(ang)[None, :, None, :]
    xf = x.astype(jnp.float32)
    x1, x2 = xf[..., :half], xf[..., half:]
    return jnp.concatenate([x1 * cos - x2 * sin, x2 * cos + x1 * sin], axis=-1).astype(x.dtype)

def apply_axial_rope(x, row, col):
    half = x.shape[-1] // 2
    xr = apply_rope(x[..., :half], rope_angles(row, half))
    xc = apply_rope(x[..., half:], rope_angles(col, half))
    return jnp.concatenate([xr, xc], axis=-1)

def window_sink_attention(q, k, v, sink):
    B, L, Hq, dh = q.shape
    Hkv = k.shape[2]
    G = Hq // Hkv
    Lp = L + PAD_FRONT
    nb = Lp // BLOCK
    scale = dh ** -0.5
    qb = jnp.pad(q, ((0, 0), (PAD_FRONT, 0), (0, 0), (0, 0))).reshape(B, nb, BLOCK, Hkv, G, dh)
    kv_pad = ((0, 0), (PAD_FRONT + BLOCK, BLOCK), (0, 0), (0, 0))
    kp = jnp.pad(k, kv_pad).reshape(B, nb + 2, BLOCK, Hkv, dh)
    vp = jnp.pad(v, kv_pad).reshape(B, nb + 2, BLOCK, Hkv, dh)
    kb = jnp.concatenate([kp[:, :-2], kp[:, 1:-1], kp[:, 2:]], axis=2)
    vb = jnp.concatenate([vp[:, :-2], vp[:, 1:-1], vp[:, 2:]], axis=2)
    q_pos = np.arange(nb)[:, None] * BLOCK + np.arange(BLOCK)[None, :]
    k_pos = (np.arange(nb)[:, None] - 1) * BLOCK + np.arange(3 * BLOCK)[None, :]
    kpb = k_pos[:, None, :]
    band = (np.abs(q_pos[:, :, None] - kpb) <= WINDOW) & (kpb >= PAD_FRONT + META) & (kpb < Lp)
    s_win = jnp.einsum('bnqhgd,bnkhd->bnhgqk', qb, kb).astype(jnp.float32) * scale
    s_win = jnp.where(band[None, :, None, None], s_win, NEG)
    km, vm = k[:, :META], v[:, :META]
    s_meta = jnp.einsum('bnqhgd,bmhd->bnhgqm', qb, km).astype(jnp.float32) * scale
    s = jnp.concatenate([s_meta, s_win], axis=-1)
    sk = sink.astype(jnp.float32).reshape(Hkv, G)[None, None, :, :, None, None]
    m = jnp.maximum(jnp.max(s, axis=-1, keepdims=True), sk)
    p = jnp.exp(s - m)
    p = (p / (jnp.sum(p, axis=-1, keepdims=True) + jnp.exp(sk - m))).astype(v.dtype)
    o = (jnp.einsum('bnhgqm,bmhd->bnqhgd', p[..., :META], vm)
         + jnp.einsum('bnhgqk,bnkhd->bnqhgd', p[..., META:], vb))
    return o.reshape(B, Lp, Hq * dh)[:, PAD_FRONT:]

def neighbourhood_attention(q, k, v, rpb):
    B, L, H, dh = q.shape
    S = L - META
    rows = S // GRID_W
    kr = min(WIN_ROWS, rows)
    ncb = GRID_W // QCOLS
    scale = dh ** -0.5
    qm, km, vm = q[:, :META], k[:, :META], v[:, :META]
    qg = q[:, META:].reshape(B, rows, ncb, QCOLS, H, dh)
    kt, vt = k[:, META:], v[:, META:]
    r = np.arange(rows)
    key_rows = np.clip(r - kr // 2, 0, rows - kr)[:, None] + np.arange(kr)[None, :]
    qcol = np.arange(ncb)[:, None] * QCOLS + np.arange(QCOLS)[None, :]
    qcol_start = np.clip(qcol - WIN_COLS // 2, 0, GRID_W - WIN_COLS)
    key_cols = (np.clip(np.arange(ncb) * QCOLS - WIN_COLS // 2, 0, GRID_W - KCOLS)[:, None]
                + np.arange(KCOLS)[None, :])
    tok = (key_rows[:, None, :, None] * GRID_W + key_cols[None, :, None, :]).reshape(rows, ncb, kr * KCOLS)
    kg = kt[:, tok]
    vg = vt[:, tok]
    col_ok = ((key_cols[:, None, :] >= qcol_start[:, :, None])
              & (key_cols[:, None, :] < qcol_start[:, :, None] + WIN_COLS))
    col_ok = np.broadcast_to(col_ok[:, :, None, :], (ncb, QCOLS, kr, KCOLS)).reshape(ncb, QCOLS, kr * KCOLS)
    dr = key_rows - r[:, None] + WIN_ROWS - 1
    dc = np.clip(key_cols[:, None, :] - qcol[:, :, None] + WIN_COLS - 1, 0, 2 * WIN_COLS - 2)
    bias = rpb[:, dr[:, None, None, :, None], dc[None, :, :, None, :]]
    bias = bias.reshape(H, rows, ncb, QCOLS, kr * KCOLS).astype(jnp.float32)
    s_win = jnp.einsum('brcqhd,brckhd->bhrcqk', qg, kg).astype(jnp.float32) * scale + bias[None]
    s_win = jnp.where(col_ok[None, None, None], s_win, NEG)
    s_meta = jnp.einsum('brcqhd,bmhd->bhrcqm', qg, km).astype(jnp.float32) * scale
    p = jax.nn.softmax(jnp.concatenate([s_meta, s_win], axis=-1), axis=-1).astype(v.dtype)
    og = (jnp.einsum('bhrcqm,bmhd->brcqhd', p[..., :META], vm)
          + jnp.einsum('bhrcqk,brckhd->brcqhd', p[..., META:], vg)).reshape(B, S, H * dh)
    sm = jnp.einsum('bmhd,bnhd->bhmn', qm, km).astype(jnp.float32) * scale
    om = jnp.einsum('bhmn,bnhd->bmhd', jax.nn.softmax(sm, axis=-1).astype(v.dtype), vm).reshape(B, META, H * dh)
    return jnp.concatenate([om, og], axis=1)

def dense_block_attention(q, k, v):
    B, L, Hq, dh = q.shape
    Hkv = k.shape[2]
    G = Hq // Hkv
    Lp = L + PAD_FRONT
    nb = Lp // BLOCK
    scale = dh ** -0.5
    pad = ((0, 0), (PAD_FRONT, 0), (0, 0), (0, 0))
    qb = jnp.pad(q, pad).reshape(B, nb, BLOCK, Hkv, G, dh)
    kp = jnp.pad(k, pad)
    vp = jnp.pad(v, pad)
    key_ok = np.arange(Lp) >= PAD_FRONT

    def one_block(qblk):
        s = jnp.einsum('bqhgd,bkhd->bhgqk', qblk, kp).astype(jnp.float32) * scale
        s = jnp.where(key_ok, s, NEG)
        p = jax.nn.softmax(s, axis=-1).astype(vp.dtype)
        return jnp.einsum('bhgqk,bkhd->bqhgd', p, vp)

    o = lax.map(one_block, jnp.moveaxis(qb, 1, 0))
    return jnp.moveaxis(o, 0, 1).reshape(B, Lp, Hq * dh)[:, PAD_FRONT:]

def hybrid_mixer(n, w_in, sink, rpb, qn, kn, w_branch, w_out, pos, row, col):
    B, L, _ = n.shape
    offsets = np.cumsum(IN_SIZES)[:-1].tolist()
    qa, ka, va, qb, kb, vb, qc, kc, vc, gates = jnp.split(n @ w_in, offsets, axis=-1)
    heads = lambda t, h: t.reshape(B, L, h, HEAD_DIM)
    ang = rope_angles(pos, HEAD_DIM)
    oa = window_sink_attention(apply_rope(heads(qa, A_Q_HEADS), ang), apply_rope(heads(ka, A_KV_HEADS), ang),
                               heads(va, A_KV_HEADS), sink)
    ob = neighbourhood_attention(heads(qb, B_HEADS), heads(kb, B_HEADS), heads(vb, B_HEADS), rpb)
    qc = apply_axial_rope(rms_norm_2(heads(qc, C_Q_HEADS), qn), row, col)
    kc = apply_axial_rope(rms_norm_2(heads(kc, C_KV_HEADS), kn), row, col)
    oc = dense_block_attention(qc, kc, heads(vc, C_KV_HEADS))
    branches = jnp.stack([oa, ob, oc], axis=2)
    up = jnp.einsum('blnc,ncd->blnd', branches, w_branch)
    g = jax.nn.sigmoid(gates.reshape(B, L, N_BRANCH, D_MODEL))
    return jnp.sum(g * up, axis=2) @ w_out

def second_inputs(seed: int = 0) -> dict:
    key = jax.random.key(seed)
    ks = jax.random.split(key, 17)
    f32 = jnp.float32

    def nrm(k, shape, scale):
        return jax.random.normal(k, shape, f32) * scale

    def gain(k, shape):
        return 1.0 + 0.02 * jax.random.normal(k, shape, f32)

    return {
        "x": nrm(ks[0], (BATCH, SEQ, D_MODEL), 1.0),
        "meta_tokens": nrm(ks[1], (META, D_MODEL), 1.0),
        "ffn1_norm": gain(ks[2], (DEPTH_2, D_MODEL)),
        "ffn1_w_in": nrm(ks[3], (DEPTH_2, D_MODEL, 2 * D_FF), D_MODEL ** -0.5),
        "ffn1_w_out": nrm(ks[4], (DEPTH_2, D_FF, D_MODEL), D_FF ** -0.5),
        "mix_norm": gain(ks[5], (DEPTH_2, D_MODEL)),
        "w_in": nrm(ks[6], (DEPTH_2, D_MODEL, N_IN_2), D_MODEL ** -0.5),
        "sink_a": nrm(ks[7], (DEPTH_2, A_Q_HEADS), 0.5),
        "rpb_b": nrm(ks[8], (DEPTH_2, B_HEADS, 2 * WIN_ROWS - 1, 2 * WIN_COLS - 1), 0.1),
        "qnorm_c": gain(ks[9], (DEPTH_2, HEAD_DIM)),
        "knorm_c": gain(ks[10], (DEPTH_2, HEAD_DIM)),
        "w_branch": nrm(ks[11], (DEPTH_2, N_BRANCH, BRANCH_WIDTH, D_MODEL), BRANCH_WIDTH ** -0.5),
        "w_out": nrm(ks[12], (DEPTH_2, D_MODEL, D_MODEL), D_MODEL ** -0.5),
        "ffn2_norm": gain(ks[13], (DEPTH_2, D_MODEL)),
        "ffn2_w_in": nrm(ks[14], (DEPTH_2, D_MODEL, 2 * D_FF), D_MODEL ** -0.5),
        "ffn2_w_out": nrm(ks[15], (DEPTH_2, D_FF, D_MODEL), D_FF ** -0.5),
        "final_norm": gain(ks[16], (D_MODEL,)),
    }

def second_block(x, meta_tokens, ffn1_norm, ffn1_w_in, ffn1_w_out, mix_norm, w_in, sink_a, rpb_b,
              qnorm_c, knorm_c, w_branch, w_out, ffn2_norm, ffn2_w_in, ffn2_w_out, final_norm):
    B, S, D = x.shape
    L = S + META
    h = jnp.concatenate([jnp.broadcast_to(meta_tokens.astype(x.dtype)[None], (B, META, D)), x], axis=1)
    p = np.arange(L)
    t = p - META
    pos = jnp.asarray(p)
    row = jnp.asarray(np.where(t >= 0, t // GRID_W, -1))
    col = jnp.asarray(np.where(t >= 0, t % GRID_W, p))
    for l in range(DEPTH_2):
        h = h + 0.5 * swiglu(rms_norm_2(h, ffn1_norm[l]), ffn1_w_in[l], ffn1_w_out[l])
        h = h + hybrid_mixer(rms_norm_2(h, mix_norm[l]), w_in[l], sink_a[l], rpb_b[l], qnorm_c[l], knorm_c[l],
                             w_branch[l], w_out[l], pos, row, col)
        h = h + 0.5 * swiglu(rms_norm_2(h, ffn2_norm[l]), ffn2_w_in[l], ffn2_w_out[l])
    return rms_norm_2(h, final_norm)[:, META:]


def setup_inputs(seed=0):
    out = dict(first_inputs(seed))
    for name, value in second_inputs(seed + 1).items():
        if name != "x":
            out[name + "_2"] = value
    return out


def reference(
    x, attn_norm_g, w_in, conv_w, conv_b, conv_ln_g, conv_ln_b, conv_pw_w, conv_pw_b, pool_w,
    pool_scale, q_norm_g, k_norm_g, lambda_q1, lambda_k1, lambda_q2, lambda_k2, attn_sub_norm_g,
    w_out, ffn_norm_g, router_g_w, router_g_b, router_e_w, router_e_b, w_gate, w_up, w_down,
    meta_tokens_2, ffn1_norm_2, ffn1_w_in_2, ffn1_w_out_2, mix_norm_2, w_in_2, sink_a_2,
    rpb_b_2, qnorm_c_2, knorm_c_2, w_branch_2, w_out_2, ffn2_norm_2, ffn2_w_in_2, ffn2_w_out_2,
    final_norm_2,
):
    x = first_block(
        x, attn_norm_g, w_in, conv_w, conv_b, conv_ln_g, conv_ln_b, conv_pw_w, conv_pw_b,
        pool_w, pool_scale, q_norm_g, k_norm_g, lambda_q1, lambda_k1, lambda_q2, lambda_k2,
        attn_sub_norm_g, w_out, ffn_norm_g, router_g_w, router_g_b, router_e_w, router_e_b,
        w_gate, w_up, w_down,
    )
    return second_block(
        x, meta_tokens_2, ffn1_norm_2, ffn1_w_in_2, ffn1_w_out_2, mix_norm_2, w_in_2, sink_a_2,
        rpb_b_2, qnorm_c_2, knorm_c_2, w_branch_2, w_out_2, ffn2_norm_2, ffn2_w_in_2,
        ffn2_w_out_2, final_norm_2,
    )


_drawn_inputs = setup_inputs


def setup_inputs(seed=0):
    import zlib

    import numpy as np

    out = dict(_drawn_inputs(seed))
    spreads = {}
    factors = {'conv_b': 3.695,
     'conv_ln_g': 4.726,
     'conv_ln_b': 7.047,
     'conv_pw_b': 3.74,
     'pool_scale': 3.844,
     'q_norm_g': 4.844,
     'k_norm_g': 4.341,
     'router_g_b': 8.0,
     'router_e_b': 8.0,
     'ffn1_norm_2': 6.122,
     'mix_norm_2': 8.0,
     'sink_a_2': 8.0,
     'rpb_b_2': 6.469,
     'qnorm_c_2': 8.0,
     'knorm_c_2': 8.0,
     'ffn2_norm_2': 6.295,
     'final_norm_2': 2.726}
    for name, (base, spread) in spreads.items():
        noise = np.random.default_rng([zlib.crc32(name.encode()), seed]).standard_normal(out[name].shape)
        drawn = base * np.exp(spread * noise) if base else spread * noise
        out[name] = __import__('jax').numpy.asarray(drawn.astype(out[name].dtype))
    for name, factor in factors.items():
        out[name] = (out[name] * factor).astype(out[name].dtype)
    return out
```

```python
from contextlib import ExitStack

import numpy as np

import concourse.bass as bass
from concourse import mybir

F32 = mybir.dt.float32
F32R = mybir.dt.float32r
I32 = mybir.dt.int32
ALU = mybir.AluOpType
ACT = mybir.ActivationFunctionType
AX = mybir.AxisListType

P = 128
D = 1024
KD = D // P
SEQ = 256
META = 16
L = SEQ + META
EPS = 1e-6
LAYERS = 2
HD = 64
FF = 2816
FT = FF // P
HEADS1 = 4
MOE_T = 4096 // P
MOE_HALF = MOE_T // 2
CONVW = 31
LAM_INIT = 0.2

BLK = 8
RING = 4
AHEAD = 3
IN1, OUT1 = 18, 8
PEEL1 = 6
MOE_C = 2 * MOE_HALF + MOE_HALF * KD // BLK
B1_CHUNKS = IN1 + OUT1 + 2 * MOE_C
FFN_UP, FFN_DOWN = 2 * FT, FT * KD // BLK
FFN_C = FFN_UP + FFN_DOWN
QKV_T, GATE_T = 24, 24
BRANCH_C, OUT_C = 3 * 4 * KD // BLK, KD
LAYER_C = 2 * FFN_C + QKV_T + GATE_T + BRANCH_C + OUT_C
CHUNKS = B1_CHUNKS + LAYERS * LAYER_C
STREAM = CHUNKS + AHEAD

B1_OUTS = IN1 + OUT1 + 2 * (2 * MOE_HALF + KD)
LAYER_O = 2 * (FFN_UP + KD) + QKV_T + GATE_T + 3 * KD + KD

R_KA, R_KC, R_KB, R_QA, R_QC, R_QB = 0, 1, 2, 6, 10, 14
QKV_ORDER = ([("kA", 0), ("kC", 0)] + [("kB", t) for t in range(4)] + [("v", t) for t in range(6)]
             + [("qA", t) for t in range(4)] + [("qC", t) for t in range(4)] + [("qB", t) for t in range(4)])
R_OF = {"kA": R_KA, "kC": R_KC, "kB": R_KB, "qA": R_QA, "qC": R_QC, "qB": R_QB}
QKV_EVENTS = {0: [("stat", 0)], 1: [("swapA", R_KA)]}
for _t in range(6):
    QKV_EVENTS[7 + _t] = [("v", _t)]
for _t in range(4):
    QKV_EVENTS[13 + _t] = [("swapA", R_QA + _t)]
C_TILES = [R_KC] + [R_QC + t for t in range(4)]
QKV_EVENTS[20] = [("sumC", 0)]
QKV_EVENTS[21] = [("castC", i) for i in range(5)]
QKV_EVENTS[22] = [("swapC", r) for r in C_TILES]
AUX_QKV = sum(len(v) for v in QKV_EVENTS.values())
LAYER_A = 2 + AUX_QKV
CASTC_IN_LAYER = 1 + sum(len(v) for t, v in QKV_EVENTS.items() if t < 21)
B1_EVENTS = ([("stat", 0), ("qk_sum", 0)] + [("qk_cast", t) for t in range(8)]
             + [("lambda", 0), ("conv_mean", 0), ("conv_var", 0)]
             + [("pointwise", i) for i in range(2)] + [("pool", i) for i in range(2)]
             + [("v", t) for t in range(HEADS1)]
             + [e for t in range(HEADS1) for e in (("score0", t), ("score1", t), ("turn", t), ("pv", t))]
             + [("o_sum", 0)] + [("o_cast", t) for t in range(HEADS1)]
             + [("stat", 1), ("router", 0), ("router_turn", 0), ("gates_turn", 0)]
             + [("gates_cast", e) for e in range(8)])
B1E = {e: i for i, e in enumerate(B1_EVENTS)}
B1_AUX = len(B1_EVENTS)
DVE_STEPS = 73

POOL_STEPS = 50

SKEW = 64 * 128

C_G = 0
C_QN = C_G + 9 * KD
C_SINK = C_QN + 2 * LAYERS
C_CONVW = C_SINK + 8 * LAYERS
C_CONVB = C_CONVW + 2 * CONVW
C_LNG, C_LNB, C_PWB = C_CONVB + 2, C_CONVB + 4, C_CONVB + 6
C_PS = C_PWB + 2
C_QN1 = C_PS + 2
C_SUB = C_QN1 + 2
C_LAM = C_SUB + 1
C_RB = C_LAM + 4
C_RW = C_RB + 1
NC = C_RW + KD * 20
M_ID, M_ONES, M_PA, M_PC = 0, P, 2 * P, 3 * P
M_SEL16 = 4 * P
M_SEL4 = 5 * P
M_TAB = M_SEL4 + 16
M_MA = M_TAB + 4 * L
M_MBM = M_MA + 3 * L
M_MB = M_MBM + L
NM = M_MB + 2 * SEQ


class Count:

    def __init__(self, start=0):
        self.n, self.term, self.stack = start, 0, []

    def up(self, k=1):
        self.n += k
        return k

    @property
    def now(self):
        return self.term + self.n

    def enter(self, i, per, first=0):
        self.stack.append((self.n, self.term, per, first))
        self.term = self.term + i * per
        self.n -= first * per

    def leave(self, turns):
        n0, term, per, first = self.stack.pop()
        assert self.n - (n0 - first * per) == per, (self.n - (n0 - first * per), per)
        self.term, self.n = term, n0 + per * turns


def build(nc, stream, xT, cols, mats, b1mats, rpbz, out):
    with ExitStack() as ctx:
        def sb(name, shape, dt=F32):
            return ctx.enter_context(nc.sbuf_tensor(name, shape, dt))

        def sem(name):
            return ctx.enter_context(nc.semaphore(name))

        raw = sb("raw", [P, RING, BLK * P])
        w_hi = sb("w_hi", [P, RING, BLK * P], F32R)
        w_lo = sb("w_lo", [P, RING, BLK * P], F32R)
        h = sb("h", [P, KD, L])
        x_hi = sb("x_hi", [P, KD, L], F32R)
        x_lo = sb("x_lo", [P, KD, L], F32R)
        a_hi = sb("a_hi", [P, FT, L], F32R)
        a_lo = sb("a_lo", [P, FT, L], F32R)
        qk = sb("qk", [P, 18, L])
        G = sb("G", [P, GATE_T, L])
        v_tok = sb("v_tok", [P, 3, 6 * P])
        S_sb = sb("S_sb", [P, 2, 3, L])
        PT = sb("PT", [P, 3, L])
        biasB = sb("biasB", [P, 2, 2, L])
        rstd = sb("rstd", [P, L])
        col = sb("col", [P, NC])
        mat = sb("mat", [P, NM])
        small = sb("small", [P, 96])
        PS = ctx.enter_context(nc.psum_tensor("PS", [P, 8, 512], F32))

        ident, ones = mat[:, M_ID:M_ID + P], mat[:, M_ONES:M_ONES + P]
        Gf = G[:, :, :].rearrange("p a b -> p (a b)")
        vstage = [G[:, 6, :], G[:, 7, :]]
        acc, sq, ms = G[:, 20, :], G[:, 21, :], G[:, 22, :]
        zero = small[:, 1:2]
        minl, rsum, rden, esink = (small[:, 4 + 8 * i:4 + 8 * i + 6] for i in range(4))
        alibi = Gf[:, 0:2048].rearrange("p (h t k) -> p h t k", h=4, t=2)
        U = Gf[:, 2048:2620].rearrange("p (i t) -> p i t", i=2)
        Y = Gf[:, 2624:3136].rearrange("p (i t) -> p i t", i=2)
        YC = Gf[:, 3136:3648].rearrange("p (i t) -> p i t", i=2)
        YS = Gf[:, 3648:4160].rearrange("p (i t) -> p i t", i=2)
        UP = Gf[:, 4160:4704].rearrange("p (i t) -> p i t", i=2)
        UW = Gf[:, 4704:5248].rearrange("p (i t) -> p i t", i=2)
        O2 = Gf[:, 2048:3072].rearrange("p (h t) -> p h t", h=4)
        PTf = PT[:, :, :].rearrange("p a b -> p (a b)")
        pool_w = PTf[:, 384:640].rearrange("p (i c) -> p i c", i=2)
        bB = biasB[:, :, :, :].rearrange("p a b c -> p (a b c)")
        invcount = bB[:, 0:512].rearrange("p (i t) -> p i t", i=2)
        pw_w = bB[:, 512:1024].rearrange("p (k c) -> p k c", k=2)
        S_f = S_sb[:, :, :, :].rearrange("p a b c -> p (a b c)")
        v_f = v_tok[:, :, :].rearrange("p a b -> p (a b)")
        gates_bc = Gf[:, 0:16 * SEQ].rearrange("p (e t) -> p e t", e=16)

        raw_landed = [sem(f"raw_landed{s}") for s in range(RING)]
        hi_done, lo_done = sem("hi_done"), sem("lo_done")
        chunk_used = sem("chunk_used")
        out_free = sem("out_free")
        aux_out, aux_free = sem("aux_out"), sem("aux_free")
        inputs_landed, consts_landed = sem("inputs_landed"), sem("consts_landed")
        x_hi_done, x_lo_done = sem("x_hi_done"), sem("x_lo_done")
        squares_summed, rstd_done = sem("squares_summed"), sem("rstd_done")
        act_done, a_ready = sem("act_done"), sem("a_ready")
        a_hi_done, a_lo_done = sem("a_hi_done"), sem("a_lo_done")
        c_squared, c_rstd, roped = sem("c_squared"), sem("c_rstd"), sem("roped")
        scores_out, logits_ready, exp_done, rden_ready = (
            sem("scores_out"), sem("logits_ready"), sem("exp_done"), sem("rden_ready"))
        probs_ready, probsT_out, probsT_dve, probsT_act = (
            sem("probs_ready"), sem("probsT_out"), sem("probsT_dve"), sem("probsT_act"))
        pv_out, o_hi_done, o_lo_done = sem("pv_out"), sem("o_hi_done"), sem("o_lo_done")
        bias_landed = [sem(f"bias_landed{i}") for i in range(2)]
        bias_ready = sem("bias_ready")
        gate_sig, mixed_ready, mix_hi_done, mix_lo_done = (
            sem("gate_sig"), sem("mixed_ready"), sem("mix_hi_done"), sem("mix_lo_done"))
        setup_done = sem("setup_done")
        dve_step, act_step, pool_step = sem("dve_step"), sem("act_step"), sem("pool_step")
        conv_gate, qk_squared, lam_exp = sem("conv_gate"), sem("qk_squared"), sem("lam_exp")
        conv_squared, conv_act, mix1_hi = sem("conv_squared"), sem("conv_act"), sem("mix1_hi")
        exp1_done, o_squared, router_exp = sem("exp1_done"), sem("o_squared"), sem("router_exp")
        lam_products, conv_done, conv_centred, conv_scaled = (
            sem("lam_products"), sem("conv_done"), sem("conv_centred"), sem("conv_scaled"))
        logits1_ready, probs1_mixed, mix1_lo = sem("logits1_ready"), sem("probs1_mixed"), sem("mix1_lo")
        router_logits, router_centred, gates_ready = sem("router_logits"), sem("router_centred"), sem("gates_ready")
        head_root, conv_root, o_root, pooled = sem("head_root"), sem("conv_root"), sem("o_root"), sem("pooled")
        out_ready = sem("out_ready")
        stored = sem("stored")

        block = ctx.enter_context(nc.Block())

        def bank(o):
            return o % 4

        def down_done(m, kt=FT):
            return (kt * (m + 1) - 1) // BLK

        def q_rows(qt):
            return P if qt < 2 else META

        def slot_of(base, c):
            return (base + c) % RING

        B2S = B1_CHUNKS % RING
        B2B = B1_OUTS % 4
        assert LAYER_C % RING == 0 and LAYER_O % 4 == 0

        def pair_hi(act, l, pr):
            act.wait_ge(pv_out, l * 24 + 2 * pr + 2)
            act.activation(a_hi[:, pr, :], PS[:, 7, 0:L], ACT.Copy).then_inc(o_hi_done, 1)

        def sig(act, ob, l, k):
            j = (k % 3) * KD + k // 3
            act.wait_ge(out_free, ob + (FFN_UP + KD + QKV_T + j + 1))
            act.activation(G[:, j, :], G[:, j, :], ACT.Sigmoid).then_inc(gate_sig, 1)

        def small_g():
            return small[:, 60:68]

        def B1S(m, qt, k):
            off = (m * 2 + qt) * SEQ
            return S_f[:, off:off + k]

        def pair_lo(dve, l, pr):
            dve.wait_ge(o_hi_done, l * 12 + pr + 1)
            dve.tensor_tensor(a_lo[:, pr, :], PS[:, 7, 0:L], a_hi[:, pr, :].bitcast(F32), ALU.subtract).then_inc(o_lo_done, 1)

        @block.sync
        def _(sp):
            sp.dma_start(h[:, :, :], xT).then_inc(inputs_landed, 16)
            sp.dma_start(col[:, :], cols).then_inc(inputs_landed, 16)
            for s in range(RING):
                sp.dma_start(raw[:, s, :], stream[s]).then_inc(raw_landed[s], 16)
            sp.dma_start(mat[:, :], mats).then_inc(consts_landed, 16)
            sp.dma_start(alibi, b1mats[:, 0:2048].rearrange("p (h t k) -> p h t k", h=4, t=2)).then_inc(consts_landed, 16)
            sp.dma_start(bB[:, 0:1024], b1mats[:, 2048:3072]).then_inc(consts_landed, 16)
            sp.dma_start(PTf[:, 384:640], b1mats[:, 3072:3328]).then_inc(consts_landed, 16)
            with sp.Fori(1, STREAM // RING) as i:
                for s in range(RING):
                    sp.wait_ge(lo_done, i * RING + (s - RING + 1))
                    sp.dma_start(raw[:, s, :], stream[i * RING + s]).then_inc(raw_landed[s], 16)
            for n in range(STREAM // RING * RING, STREAM):
                sp.wait_ge(lo_done, n - RING + 1)
                sp.dma_start(raw[:, n % RING, :], stream[n]).then_inc(raw_landed[n % RING], 16)
            for m in range(KD):
                sp.wait_ge(out_ready, m + 1)
                sp.dma_start(out[:, m, :], qk[:, m, 0:SEQ]).then_inc(stored, 16)
            sp.wait_ge(stored, 16 * KD)

        ALL_CONSTS = 16 * 4

        @block.scalar
        def _(act):
            def split_hi(n, slot):
                if isinstance(n, int):
                    act.wait_ge(raw_landed[slot], 16 * (n // RING + 1))
                    if n >= RING:
                        act.wait_ge(chunk_used, n - RING + 1)
                else:
                    act.wait_ge(raw_landed[slot], 4 * n + (16 - 4 * slot))
                    act.wait_ge(chunk_used, n - (RING - 1))
                act.activation(w_hi[:, slot, :], raw[:, slot, :], ACT.Copy).then_inc(hi_done, 1)

            def norm_hi(v, m, o):
                act.wait_ge(out_free, o + 1)
                act.activation(x_hi[:, m, :], h[:, m, :], ACT.Copy,
                               scale=col[:, bass.ds(C_G + v * KD + m, 1)]).then_inc(x_hi_done, 1)

            ff = Count()

            def ffn_up(c0, slot0, o, tiles, n_tok):
                def finish(b, f, k):
                    act.wait_ge(a_ready, ff.now + k)
                    act.activation(a_hi[:, bass.ds(f, 1), 0:n_tok], S_sb[:, b, 2:3, 0:n_tok], ACT.Copy)\
                       .then_inc(a_hi_done, 1)

                def turn(c, o, f, first):
                    for s in range(4):
                        split_hi(c + (s + AHEAD), (slot0 + s + AHEAD) % RING)
                        if s == 0 and not first:
                            finish(1, f - 1, 0)
                        if s == 2:
                            finish(0, f, 1)
                        if s % 2 == 1:
                            act.wait_ge(out_free, o + s)
                            act.activation(S_sb[:, s // 2, 0, 0:n_tok], S_sb[:, s // 2, 0, 0:n_tok], ACT.Silu).then_inc(act_done, 1)
                    ff.up(2)

                turn(c0, o, 0, True)
                with act.Fori(1, tiles // 2) as i:
                    ff.enter(i, 2, 1)
                    turn(c0 + i * 4, o + i * 4, i * 2, False)
                    ff.leave(tiles // 2 - 1)
                finish(1, tiles - 1, 0)

            def down(c0, slot0, o, kt, v):
                for c in range(kt * KD // BLK):
                    split_hi(c0 + (c + AHEAD), (slot0 + c + AHEAD) % RING)
                    for m in range(KD):
                        if down_done(m, kt) == c and v is not None:
                            norm_hi(v, m, o + m)

            for n in range(AHEAD):
                split_hi(n, n)
            act.wait_ge(inputs_landed, 32)
            for m in range(KD):
                act.activation(x_hi[:, m, :], h[:, m, :], ACT.Copy,
                               scale=col[:, C_G + m:C_G + m + 1]).then_inc(x_hi_done, 1)

            for c in range(PEEL1):
                split_hi(c + AHEAD, (c + AHEAD) % RING)
            with act.Fori(0, (IN1 - PEEL1) // 4) as i:
                for s in range(4):
                    split_hi(i * 4 + (PEEL1 + s + AHEAD), (PEEL1 + s + AHEAD) % RING)
            act.wait_ge(out_free, IN1)
            for i in range(2):
                act.activation(qk[:, 2 + i, 0:SEQ], qk[:, 2 + i, 0:SEQ], ACT.Sigmoid).then_inc(conv_gate, 1)
            for t in range(8):
                act.activation(v_f[:, t * SEQ:(t + 1) * SEQ], qk[:, 6 + t, 0:SEQ], ACT.Square).then_inc(qk_squared, 1)
            act.wait_ge(aux_free, B1E["lambda", 0] + 1)
            act.activation(small[:, 42:44], small[:, 40:42], ACT.Exp).then_inc(lam_exp, 1)
            act.wait_ge(conv_centred, 1)
            act.activation(YS[:, 0, :], YC[:, 0, :], ACT.Square).then_inc(conv_squared, 1)
            act.wait_ge(aux_free, B1E["conv_mean", 0] + 1)
            act.activation(YS[:, 1, :], YC[:, 1, :], ACT.Square).then_inc(conv_squared, 1)
            for i in range(2):
                act.wait_ge(conv_scaled, i + 1)
                act.activation(Y[:, i, :], YC[:, i, :], ACT.Silu, scale=col[:, C_LNG + i:C_LNG + i + 1],
                               bias=col[:, C_LNB + i:C_LNB + i + 1]).then_inc(conv_act, 1)
            for i in range(2):
                k = B1E["pointwise", i]
                act.wait_ge(aux_out, k + 1)
                act.activation(a_hi[:, i, 0:SEQ], PS[:, 4 + k % 4, 0:SEQ], ACT.Identity,
                               bias=col[:, C_PWB + i:C_PWB + i + 1]).then_inc(mix1_hi, 1)
            for i in range(2):
                k = B1E["pool", i]
                act.wait_ge(aux_out, k + 1)
                act.activation(a_hi[:, 2 + i, 0:SEQ], PS[:, 4 + k % 4, 0:SEQ], ACT.Copy,
                               scale=col[:, C_PS + i:C_PS + i + 1]).then_inc(mix1_hi, 1)
            for hd in range(HEADS1):
                for m in range(2):
                    for qt in range(2):
                        if qt == 0:
                            act.wait_ge(logits1_ready, 2 * hd + m + 1)
                        else:
                            act.wait_ge(aux_free, B1E[f"score{m}", hd] + 1)
                        k, e = (qt + 1) * P, 2 * m + qt
                        act.activation(B1S(m, qt, k), B1S(m, qt, k), ACT.Exp, scale=-1.0, bias=small[:, 48 + e:49 + e],
                                       accum_out=small[:, 52 + e:53 + e]).then_inc(exp1_done, 1)
            for t in range(HEADS1):
                act.wait_ge(aux_free, B1E["pv", t] + 1)
                act.activation(O2[:, t, :], qk[:, t, 0:SEQ], ACT.Square).then_inc(o_squared, 1)
            for t in range(HEADS1):
                act.wait_ge(aux_free, B1E["o_cast", t] + 1)
                act.activation(a_hi[:, 4 + t, 0:SEQ], qk[:, t, 0:SEQ], ACT.Copy).then_inc(mix1_hi, 1)
            for c in range(OUT1):
                split_hi(IN1 + c + AHEAD, (IN1 + c + AHEAD) % RING)
                norm_hi(1, c, IN1 + c)
            act.wait_ge(router_centred, 1)
            act.activation(small_g(), small_g(), ACT.Exp).then_inc(router_exp, 1)
            act.wait_ge(router_centred, 2)
            act.activation(small[:, 90:92], small[:, 90:92], ACT.Exp).then_inc(router_exp, 1)
            cb, ob = IN1 + OUT1, IN1 + OUT1
            for half in range(2):
                ffn_up(cb, cb % RING, ob, MOE_HALF, SEQ)
                down(cb + 2 * MOE_HALF, (cb + 2 * MOE_HALF) % RING, ob + 2 * MOE_HALF, MOE_HALF, 2 if half else None)
                cb += MOE_C
                ob += 2 * MOE_HALF + KD

            with act.Fori(0, LAYERS) as l:
                cb = l * LAYER_C + B1_CHUNKS
                ob = l * LAYER_O + B1_OUTS
                sl, bk = B2S, 0
                ff.enter(l, 2 * FT)
                ffn_up(cb, sl, ob, FT, L)
                down(cb + FFN_UP, (sl + FFN_UP) % RING, ob + FFN_UP, FT, l * 3 + 3)
                c, o = FFN_C, FFN_UP + KD
                for t, (kind, i) in enumerate(QKV_ORDER):
                    split_hi(cb + (c + t + AHEAD), (sl + c + t + AHEAD) % RING)
                    if kind in ("kC", "qC"):
                        e = 0 if kind == "kC" else 1 + i
                        act.wait_ge(out_free, ob + (o + t + 1))
                        act.activation(G[:, e, :], qk[:, R_OF[kind] + i, :], ACT.Square).then_inc(c_squared, 1)
                c, o = c + QKV_T, o + QKV_T
                nexp = Count()

                def turned(j):
                    act.wait_ge(probsT_out, l * 24 + j + 1)
                    act.activation(PT[:, 1, :], PS[:, 6, 0:L], ACT.Copy).then_inc(probsT_act, 1)
                    act.activation(PT[0:META, 2, P:2 * P], PS[0:META, 6, L:L + P], ACT.Copy).then_inc(probsT_act, 1)

                for j in range(24):
                    split_hi(cb + (c + j + AHEAD), (sl + c + j + AHEAD) % RING)
                    if 7 <= j < 15:
                        if j >= 9:
                            act.wait_ge(logits_ready, l * 72 + 3 * (j - 1) + 3)
                        hB = j - 7
                        for r in range(4):
                            src = bass.AP(rpbz.tensor, l * (8 * 7 * SKEW) + ((hB * 7 + 3 - r) * SKEW + 63),
                                          [[127, 64], [SKEW, 4], [1, 64]])
                            p0 = 64 * (r % 2)
                            act.dma_start(biasB[p0:p0 + 64, hB % 2, r // 2, 0:SEQ].rearrange("p (a b) -> p a b", a=4),
                                          src).then_inc(bias_landed[hB % 2], 16)
                    for qt in range(3):
                        r = q_rows(qt)
                        act.wait_ge(logits_ready, l * 72 + 3 * j + qt + 1)
                        act.activation(S_sb[0:r, j % 2, qt, :], S_sb[0:r, j % 2, qt, :], ACT.Exp, scale=-1.0,
                                       bias=minl[0:r, 3 * (j % 2) + qt:3 * (j % 2) + qt + 1],
                                       accum_out=rsum[0:r, 3 * (j % 2) + qt:3 * (j % 2) + qt + 1]).then_inc(exp_done, nexp.up())
                    if j < 8:
                        hA = j // 2 + 4 * (j % 2)
                        act.activation(esink[:, 3 * (j % 2):3 * (j % 2) + 3], minl[:, 3 * (j % 2):3 * (j % 2) + 3], ACT.Exp,
                                       bias=col[:, bass.ds(l * 8 + C_SINK + hA, 1)]).then_inc(exp_done, nexp.up())
                    if j > 0:
                        turned(j - 1)
                    if j % 2 == 1 and j > 1:
                        pair_hi(act, l, (j - 3) // 2)
                turned(23)
                pair_hi(act, l, 11)
                assert nexp.n == 80
                for k in range(3):
                    sig(act, ob, l, k)
                c, o = c + GATE_T, o + GATE_T
                done = 3
                for s in range(BRANCH_C):
                    split_hi(cb + (c + s + AHEAD), (sl + c + s + AHEAD) % RING)
                    while done < min(24, 2 * s + 5):
                        sig(act, ob, l, done)
                        done += 1
                    for u in (2 * s, 2 * s + 1):
                        if u % 3 == 2:
                            m = u // 3
                            act.wait_ge(mixed_ready, l * KD + m + 1)
                            act.activation(a_hi[:, 12 + m, :], S_sb[:, m % 2, 0, :], ACT.Copy).then_inc(mix_hi_done, 1)
                c, o = c + BRANCH_C, o + 3 * KD
                for m in range(OUT_C):
                    split_hi(cb + (c + m + AHEAD), (sl + c + m + AHEAD) % RING)
                    norm_hi(l * 3 + 4, m, ob + (o + m))
                c, o = c + OUT_C, o + KD
                ffn_up(cb + c, (sl + c) % RING, ob + o, FT, L)
                down(cb + (c + FFN_UP), (sl + c + FFN_UP) % RING, ob + (o + FFN_UP), FT, l * 3 + 5)
                ff.leave(LAYERS)

        @block.tensor
        def _(pe):
            ax = Count()

            def aux_begin():
                k = ax.n
                if not (isinstance(ax.now, int) and k < 4):
                    pe.wait_ge(aux_free, ax.now - 3)
                return 4 + k % 4

            def aux_end(mm):
                mm.then_inc(aux_out, ax.up())

            def product(ps, slot, b, rh, rl, first, last):
                hi, lo = w_hi[:, slot, b * P:(b + 1) * P], w_lo[:, slot, b * P:(b + 1) * P]
                pe.matmul(ps, hi, rh, start=first, stop=False)
                pe.matmul(ps, hi, rl, start=False, stop=False)
                return pe.matmul(ps, lo, rh, start=False, stop=last)

            def chunk8(n, slot, o, bk, n_tok, xh, xl, ready=None, lag=4):
                pe.wait_ge(lo_done, n + 1)
                if not isinstance(o, int) or o >= lag:
                    pe.wait_ge(out_free, o - (lag - 1))
                ps = PS[:, bk, 0:n_tok]
                for kt in range(KD):
                    if ready is not None:
                        pe.wait_ge(ready[0], ready[1] + (kt + 1))
                    mm = product(ps, slot, kt, xh[:, kt, 0:n_tok], xl[:, kt, 0:n_tok], kt == 0, kt == KD - 1)
                mm.then_inc(chunk_used, 1)

            def stat(v):
                b = aux_begin()
                pe.wait_ge(squares_summed, v + 1)
                aux_end(pe.matmul(PS[:, b, 0:L], ones, acc, start=True, stop=True))

            def ffn_up(cb, slot0, ob, bk0, tiles, n_tok, v=None):
                def turn(c, o, first):
                    for s in range(4):
                        chunk8(c + s, (slot0 + s) % RING, o + s, (bk0 + s) % 4, n_tok, x_hi, x_lo,
                               (x_lo_done, v * KD) if first and s == 0 and v is not None else None)
                        if first and s == 0 and v is not None:
                            stat(v)
                turn(cb, ob, True)
                with pe.Fori(1, tiles // 2) as i:
                    turn(cb + i * 4, ob + i * 4, False)

            def down(cb, slot0, ob, bk0, kt, n_tok, abase):
                blk = 0
                for m in range(KD):
                    for k in range(kt):
                        c, b = blk // BLK, blk % BLK
                        if b == 0:
                            pe.wait_ge(lo_done, cb + (c + 1))
                        if k == 0:
                            pe.wait_ge(out_free, ob + (m - 3))
                        if m == 0:
                            pe.wait_ge(a_lo_done, abase + (k + 1))
                        mm = product(PS[:, (bk0 + m) % 4, 0:n_tok], (slot0 + c) % RING, b,
                                     a_hi[:, k, 0:n_tok], a_lo[:, k, 0:n_tok], k == 0, k == kt - 1)
                        if b == BLK - 1:
                            mm.then_inc(chunk_used, 1)
                        blk += 1

            for c in range(PEEL1):
                chunk8(c, c % RING, c, bank(c), SEQ, x_hi, x_lo, (x_lo_done, 0) if c == 0 else None)
                if c == 0:
                    pe.wait_ge(consts_landed, ALL_CONSTS)
                    stat(0)
            with pe.Fori(0, (IN1 - PEEL1) // 4) as i:
                for s in range(4):
                    c = i * 4 + (PEEL1 + s)
                    chunk8(c, (PEEL1 + s) % RING, c, bank(PEEL1 + s), SEQ, x_hi, x_lo)
            b = aux_begin()
            pe.wait_ge(qk_squared, 8)
            for t in range(8):
                mm = pe.matmul(PS[0:16, b, 0:SEQ], mat[:, M_SEL16 + 16 * t:M_SEL16 + 16 * t + 16],
                               v_f[:, t * SEQ:(t + 1) * SEQ], start=(t == 0), stop=(t == 7))
            aux_end(mm)
            pe.wait_ge(head_root, 1)
            for t in range(8):
                b = aux_begin()
                for u in range(2):
                    mm = pe.matmul(PS[64 * u:64 * u + 64, b, 0:SEQ],
                                   ident[0:16, 2 * t + u:2 * t + u + 1].to_broadcast([16, 64]),
                                   S_f[0:16, 256:512], start=True, stop=True)
                aux_end(mm)
            b = aux_begin()
            pe.wait_ge(lam_products, 1)
            aux_end(pe.matmul(PS[:, b, 0:2], ones[0:64, :], small[0:64, 38:40], start=True, stop=True))
            b = aux_begin()
            for i in range(2):
                pe.wait_ge(conv_done, i + 1)
                mm = pe.matmul(PS[:, b, 0:SEQ], ones, Y[:, i, :], start=(i == 0), stop=(i == 1))
            aux_end(mm)
            b = aux_begin()
            for i in range(2):
                pe.wait_ge(conv_squared, i + 1)
                mm = pe.matmul(PS[:, b, 0:SEQ], ones, YS[:, i, :], start=(i == 0), stop=(i == 1))
            aux_end(mm)
            pe.wait_ge(conv_act, 2)
            for m in range(2):
                b = aux_begin()
                for k in range(2):
                    mm = pe.matmul(PS[:, b, 0:SEQ], pw_w[:, k, m * P:(m + 1) * P], Y[:, k, :], start=(k == 0), stop=(k == 1))
                aux_end(mm)
            pe.wait_ge(pooled, 1)
            for m in range(2):
                b = aux_begin()
                aux_end(pe.matmul(PS[:, b, 0:SEQ], pool_w[:, m, :], qk[:, 4 + m, 0:SEQ], start=True, stop=True))
            for t in range(HEADS1):
                b = aux_begin()
                for kt in range(2):
                    mm = pe.transpose(PS[:, b, kt * P:(kt + 1) * P], qk[:, 14 + t, kt * P:(kt + 1) * P], ident)
                aux_end(mm)
            pe.wait_ge(aux_free, B1E["qk_cast", 7] + 1)
            for hd in range(HEADS1):
                for m in range(2):
                    b = aux_begin()
                    o = 64 * m
                    pe.matmul(PS[:, b, 0:P], qk[o:o + 64, 6 + hd, 0:P], qk[o:o + 64, 10 + hd, 0:P], start=True, stop=True)
                    aux_end(pe.matmul(PS[:, b, P:3 * P], qk[o:o + 64, 6 + hd, P:2 * P], qk[o:o + 64, 10 + hd, 0:SEQ],
                                      start=True, stop=True))
                b = aux_begin()
                pe.wait_ge(probs1_mixed, 2 * hd + 2)
                pe.transpose(PS[:, b, 0:P], B1S(0, 0, P), ident)
                pe.transpose(PS[:, b, P:2 * P], B1S(0, 1, P), ident)
                aux_end(pe.transpose(PS[:, b, 2 * P:3 * P], B1S(0, 1, SEQ)[:, P:2 * P], ident))
                b = aux_begin()
                pe.wait_ge(aux_free, B1E["turn", hd] + 1)
                pe.matmul(PS[:, b, 0:SEQ], v_tok[:, 0, hd * P:(hd + 1) * P], PTf[:, 0:SEQ], start=True, stop=True,
                          skip_group_check=True)
                aux_end(pe.matmul(PS[:, b, P:SEQ], v_tok[:, 1, hd * P:(hd + 1) * P], PTf[:, SEQ:SEQ + P],
                                  start=False, stop=True, skip_group_check=True))
            b = aux_begin()
            pe.wait_ge(o_squared, 4)
            for t in range(HEADS1):
                mm = pe.matmul(PS[0:4, b, 0:SEQ], mat[:, M_SEL4 + 4 * t:M_SEL4 + 4 * t + 4], O2[:, t, :],
                               start=(t == 0), stop=(t == 3))
            aux_end(mm)
            pe.wait_ge(o_root, 1)
            for t in range(HEADS1):
                b = aux_begin()
                aux_end(pe.matmul(PS[:, b, 0:SEQ], ident[0:4, t:t + 1].to_broadcast([4, P]), S_f[0:4, 256:512],
                                  start=True, stop=True))
            for c in range(OUT1):
                n = IN1 + c
                if c == 0:
                    pe.wait_ge(aux_free, B1E["pool", 1] + 1)
                    pe.wait_ge(mix1_lo, HEADS1)
                chunk8(n, n % RING, n, bank(n), SEQ, a_hi, a_lo)
            stat(1)
            b = aux_begin()
            for k in range(KD):
                pe.wait_ge(out_free, IN1 + k + 1)
                pe.wait_ge(x_lo_done, KD + k + 1)
                mm = pe.matmul(PS[0:20, b, 0:SEQ], col[:, C_RW + 20 * k:C_RW + 20 * k + 20], qk[:, 8 + k, 0:SEQ],
                               start=(k == 0), stop=(k == KD - 1))
            aux_end(mm)
            b = aux_begin()
            pe.wait_ge(router_logits, 1)
            for t in range(2):
                mm = pe.transpose(PS[:, b, 20 * t:20 * t + 20], S_f[0:20, t * P:(t + 1) * P], ident[0:20, 0:20])
            aux_end(mm)
            b = aux_begin()
            pe.wait_ge(gates_ready, 2)
            for t in range(2):
                mm = pe.transpose(PS[0:16, b, t * P:(t + 1) * P], S_f[:, 600 + 16 * t:616 + 16 * t], ident)
            aux_end(mm)
            pe.wait_ge(aux_free, B1E["gates_turn", 0] + 1)
            for e in range(8):
                b = aux_begin()
                for u in range(2):
                    mm = pe.matmul(PS[:, b, u * SEQ:(u + 1) * SEQ],
                                   ident[0:16, 2 * e + u:2 * e + u + 1].to_broadcast([16, P]),
                                   S_f[0:16, 256:512], start=True, stop=True)
                aux_end(mm)
            assert ax.n == B1_AUX, (ax.n, B1_AUX)
            cb, ob, ab = IN1 + OUT1, IN1 + OUT1, 0
            for half in range(2):
                ffn_up(cb, cb % RING, ob, bank(ob), MOE_HALF, SEQ)
                down(cb + 2 * MOE_HALF, (cb + 2 * MOE_HALF) % RING, ob + 2 * MOE_HALF, bank(ob + 2 * MOE_HALF),
                     MOE_HALF, SEQ, ab)
                cb += MOE_C
                ob += 2 * MOE_HALF + KD
                ab += MOE_HALF

            castC_at = B1_AUX + CASTC_IN_LAYER
            with pe.Fori(0, LAYERS) as l:
                ax.enter(l, LAYER_A)
                cb = l * LAYER_C + B1_CHUNKS
                ob = l * LAYER_O + B1_OUTS
                sl, bk = B2S, B2B
                ab = l * (2 * FT) + MOE_T
                ffn_up(cb, sl, ob, bk, FT, L, l * 3 + 2)
                down(cb + FFN_UP, (sl + FFN_UP) % RING, ob + FFN_UP, (bk + FFN_UP) % 4, FT, L, ab)
                c, o = FFN_C, FFN_UP + KD
                nv = 0
                for t, (kind, i) in enumerate(QKV_ORDER):
                    chunk8(cb + (c + t), (sl + c + t) % RING, ob + (o + t), (bk + o + t) % 4, L, x_hi, x_lo,
                           (x_lo_done, (l * 3 + 3) * KD) if t == 0 else None)
                    for what, i in QKV_EVENTS.get(t, []):
                        if what == "stat":
                            stat(l * 3 + 3)
                            continue
                        b = aux_begin()
                        if what in ("swapA", "swapC"):
                            if what == "swapA":
                                tt = 0 if i == R_KA else 12 + i - R_QA
                                pe.wait_ge(out_free, ob + (o + tt + 1))
                            else:
                                pe.wait_ge(aux_free, ax.term + (castC_at + C_TILES.index(i) + 1))
                            perm = mat[:, M_PA:M_PA + P] if what == "swapA" else mat[:, M_PC:M_PC + P]
                            mm = pe.matmul(PS[:, b, 0:L], perm, qk[:, i, :], start=True, stop=True)
                        elif what == "v":
                            pe.wait_ge(out_free, ob + (o + 6 + i + 1))
                            vs = vstage[i % 2]
                            pe.transpose(PS[:, b, 0:P], vs[:, 0:P], ident)
                            pe.transpose(PS[:, b, P:2 * P], vs[:, P:2 * P], ident)
                            mm = pe.transpose(PS[0:META, b, 2 * P:3 * P], vs[:, 2 * P:L], ident)
                        elif what == "sumC":
                            pe.wait_ge(c_squared, l * 5 + 5)
                            for e in range(5):
                                mm = pe.matmul(PS[0:10, b, 0:L], mat[:, M_SEL16 + 16 * e:M_SEL16 + 16 * e + 10],
                                               G[:, e, :], start=(e == 0), stop=(e == 4))
                        else:
                            pe.wait_ge(c_rstd, l + 1)
                            for u in range(2):
                                mm = pe.matmul(PS[64 * u:64 * u + 64, b, 0:L],
                                               ident[0:10, 2 * i + u:2 * i + u + 1].to_broadcast([10, 64]),
                                               G[0:10, 9, :], start=True, stop=True)
                        aux_end(mm)
                c, o = c + QKV_T, o + QKV_T
                pe.wait_ge(out_free, ob + o)
                pe.wait_ge(aux_free, ax.now)
                pe.wait_ge(roped, l * 10 + 10)

                def pv(j):
                    t, b = j // 2 % 4, j % 2
                    typ = j // 8
                    vcol = (2 + t if typ == 1 else (0 if typ == 0 else 1)) * P + 64 * b
                    pe.wait_ge(probsT_dve, l * 72 + 3 * j + 3)
                    pe.wait_ge(probsT_act, l * 48 + 2 * j + 2)
                    if b == 0 and j > 0:
                        pe.wait_ge(o_lo_done, l * 12 + j // 2)
                    for kt in range(3):
                        r = q_rows(kt)
                        mm = pe.matmul(PS[64 * b:64 * b + 64, 7, 0:L], v_tok[0:r, kt, vcol:vcol + 64], PT[0:r, kt, :],
                                       start=(kt == 0), stop=(kt == 2))
                    mm.then_inc(pv_out, 1)

                def turn(j):
                    for n, (kt, qt) in enumerate([(0, 0), (0, 1), (1, 0), (0, 2), (1, 1), (1, 2)]):
                        r = q_rows(qt)
                        if n < 3:
                            pe.wait_ge(probs_ready, l * 72 + 3 * j + n + 1)
                        pe.transpose(PS[:, 5 + kt, qt * P:qt * P + r], S_sb[0:r, j % 2, qt, kt * P:(kt + 1) * P],
                                     ident[0:r, 0:r])
                    pe.transpose(PS[0:META, 5, L:L + P], S_sb[:, j % 2, 0, 2 * P:L], ident)
                    pe.transpose(PS[0:META, 6, L:L + P], S_sb[:, j % 2, 1, 2 * P:L], ident)
                    pe.transpose(PS[0:META, 5, L + P:L + P + META], S_sb[0:META, j % 2, 2, 2 * P:L],
                                 ident[0:META, 0:META]).then_inc(probsT_out, 1)

                for j in range(24):
                    t, b = j // 2 % 4, j % 2
                    typ = j // 8
                    rq = (R_QA, R_QB, R_QC)[typ] + t
                    rk = (R_KA, R_KB + t, R_KC)[typ]
                    lo, hi = 64 * b, 64 * b + 64
                    if j > 0:
                        pe.wait_ge(logits_ready, l * 72 + 3 * j)
                    for qt in range(3):
                        r = q_rows(qt)
                        pe.matmul(PS[0:r, 2 + qt, 0:L], qk[lo:hi, rq, qt * P:qt * P + r], qk[lo:hi, rk, :],
                                  start=True, stop=True).then_inc(scores_out, 1)
                    if j > 0:
                        turn(j - 1)
                    chunk8(cb + (c + j), (sl + c + j) % RING, ob + (o + j), j % 2, L, x_hi, x_lo, lag=2)
                    if j > 0:
                        pv(j - 1)
                turn(23)
                pv(23)
                c, o = c + GATE_T, o + GATE_T
                pe.wait_ge(out_free, ob + o)
                for u in range(3 * KD):
                    s = u // 2
                    if u % 2 == 0:
                        pe.wait_ge(lo_done, cb + (c + s + 1))
                    pe.wait_ge(out_free, ob + (o + u - 3))
                    n = u % 3
                    if u < 3:
                        pe.wait_ge(o_lo_done, l * 12 + 4 * n + 4)
                    for k in range(4):
                        mm = product(PS[:, (bk + o + u) % 4, 0:L], (sl + c + s) % RING, 4 * (u % 2) + k,
                                     a_hi[:, 4 * n + k, :], a_lo[:, 4 * n + k, :], k == 0, k == 3)
                    if u % 2 == 1:
                        mm.then_inc(chunk_used, 1)
                c, o = c + BRANCH_C, o + 3 * KD
                for m in range(OUT_C):
                    chunk8(cb + (c + m), (sl + c + m) % RING, ob + (o + m), (bk + o + m) % 4, L,
                           a_hi[:, 12:20, :], a_lo[:, 12:20, :], (mix_lo_done, l * KD) if m == 0 else None)
                c, o = c + OUT_C, o + KD
                ffn_up(cb + c, (sl + c) % RING, ob + o, (bk + o) % 4, FT, L, l * 3 + 4)
                down(cb + (c + FFN_UP), (sl + c + FFN_UP) % RING, ob + (o + FFN_UP), (bk + o + FFN_UP) % 4, FT, L, ab + FT)
                ax.leave(LAYERS)
            stat(8)

        @block.vector
        def _(dve):
            st = Count()
            ax = Count()

            def step(ins):
                ins.then_inc(dve_step, st.up())
                dve.wait_ge(dve_step, st.now)

            def split_lo(n, slot):
                dve.wait_ge(hi_done, n + 1)
                dve.tensor_tensor(w_lo[:, slot, :], raw[:, slot, :], w_hi[:, slot, :].bitcast(F32),
                                  ALU.subtract).then_inc(lo_done, 1)

            def norm_lo(v, m):
                dve.wait_ge(x_hi_done, v * KD + (m + 1))
                dve.scalar_tensor_tensor(x_lo[:, m, :], h[:, m, :], col[:, bass.ds(C_G + v * KD + m, 1)],
                                         x_hi[:, m, :].bitcast(F32), ALU.mult, ALU.subtract).then_inc(x_lo_done, 1)

            def aux_bank():
                dve.wait_ge(aux_out, ax.now + 1)
                return 4 + ax.n % 4

            def inverse_root(x, y, done, k):
                n, r = x.shape[1], x.shape[0]
                t0, t1 = G[0:r, 21, 0:n], G[0:r, 23, 0:n]
                dve.wait_ge(aux_free, ax.now)
                step(dve.tensor_scalar(t0.bitcast(I32), x.bitcast(I32), 1, None, ALU.logical_shift_right))
                step(dve.tensor_scalar(y.bitcast(I32), t0.bitcast(I32), -1.0, float(0x5F3759DF), ALU.mult, ALU.add))
                for i in range(3):
                    step(dve.tensor_tensor(t0, y, y, ALU.mult))
                    step(dve.scalar_tensor_tensor(t1, t0, -0.5, x, ALU.mult, ALU.mult))
                    ins = dve.scalar_tensor_tensor(y, t1, 1.5, y, ALU.add, ALU.mult)
                    if i < 2:
                        step(ins)
                    else:
                        ins.then_inc(done, k)

            def mean_square(v):
                b = aux_bank()
                dve.tensor_scalar(ms, PS[:, b, 0:L], 1.0 / D, EPS, ALU.mult, ALU.add).then_inc(aux_free, ax.up())
                inverse_root(ms, rstd[:, :], rstd_done, 1)
                dve.wait_ge(rstd_done, v + 1)

            def residual(v, m, o, bk, coef, n_tok):
                dve.scalar_tensor_tensor(h[:, m, 0:n_tok], PS[:, bk, 0:n_tok], coef, h[:, m, 0:n_tok],
                                         ALU.mult, ALU.add).then_inc(out_free, 1)
                if v is not None:
                    dve.wait_ge(out_free, o + 1)
                    norm_lo(v, m)

            ff = Count()

            def ffn_up(cb, slot0, ob, bk0, tiles, n_tok, v=None, experts=None):
                def finish(b, f, k):
                    dve.wait_ge(a_hi_done, ff.now + k)
                    dve.tensor_tensor(a_lo[:, bass.ds(f, 1), 0:n_tok], S_sb[:, b, 2:3, 0:n_tok],
                                      a_hi[:, bass.ds(f, 1), 0:n_tok].bitcast(F32), ALU.subtract).then_inc(a_lo_done, 1)

                def turn(c, o, i, first):
                    f = i * 2
                    for s in range(4):
                        split_lo(c + (s + AHEAD), (slot0 + s + AHEAD) % RING)
                        if s == 0 and not first:
                            finish(1, f - 1, 0)
                        if s == 2:
                            finish(0, f, 1)
                        if first and s == 0 and v is not None:
                            mean_square(v)
                        b = s // 2
                        dve.wait_ge(chunk_used, c + (s + 1))
                        ps = PS[:, (bk0 + s) % 4, 0:n_tok]
                        if s % 2 == 0:
                            dve.tensor_tensor(S_sb[:, b, 0, 0:n_tok], ps, rstd[:, 0:n_tok], ALU.mult).then_inc(out_free, 1)
                            continue
                        scale = rstd[:, 0:n_tok] if experts is None else gates_bc[:, bass.ds(i + experts, 1), :]
                        up = S_sb[:, b, 1:2, 0:n_tok]
                        if experts is None:
                            dve.tensor_tensor(S_sb[:, b, 1, 0:n_tok], ps, scale, ALU.mult).then_inc(out_free, 1)
                        else:
                            dve.tensor_tensor(up, PS[:, (bk0 + s) % 4:(bk0 + s) % 4 + 1, 0:n_tok], scale, ALU.mult).then_inc(out_free, 1)
                        dve.wait_ge(out_free, o + (s + 1))
                        dve.wait_ge(act_done, ff.now + (b + 1))
                        dve.tensor_tensor(S_sb[:, b, 2, 0:n_tok], S_sb[:, b, 0, 0:n_tok], S_sb[:, b, 1, 0:n_tok],
                                          ALU.mult).then_inc(a_ready, 1)
                    ff.up(2)
                turn(cb, ob, 0, True)
                with dve.Fori(1, tiles // 2) as i:
                    ff.enter(i, 2, 1)
                    turn(cb + i * 4, ob + i * 4, i, False)
                    ff.leave(tiles // 2 - 1)
                finish(1, tiles - 1, 0)

            def down(cb, slot0, ob, bk0, kt, coef, v, n_tok):
                for c in range(kt * KD // BLK):
                    split_lo(cb + (c + AHEAD), (slot0 + c + AHEAD) % RING)
                    for m in range(KD):
                        if down_done(m, kt) == c:
                            dve.wait_ge(chunk_used, cb + (c + 1))
                            residual(v, m, ob + m, (bk0 + m) % 4, coef, n_tok)

            dve.memset(small[:, :], 0.0).then_inc(dve_step, st.up())
            dve.wait_ge(dve_step, st.now)
            step(dve.memset(small[:, 12:36], 1.0))
            step(dve.memset(U[:, :, 0:CONVW - 1], 0.0))
            step(dve.memset(UP[:, :, 0:16], 0.0))
            dve.memset(zero, 0.0).then_inc(setup_done, 1)
            for n in range(AHEAD):
                split_lo(n, n)
            dve.wait_ge(inputs_landed, 32)
            for m in range(KD):
                norm_lo(0, m)

            def in_tile(t, bk, chunk):
                dve.wait_ge(chunk_used, chunk + 1)
                dve.tensor_tensor(qk[:, bass.ds(t, 1), 0:SEQ], PS[:, bk:bk + 1, 0:SEQ],
                                  rstd[:, 0:SEQ].unsqueeze(1), ALU.mult).then_inc(out_free, 1)

            for c in range(PEEL1):
                split_lo(c + AHEAD, (c + AHEAD) % RING)
                if c == 0:
                    mean_square(0)
                in_tile(c, bank(c), c)
            with dve.Fori(0, (IN1 - PEEL1) // 4) as i:
                for s in range(4):
                    c = i * 4 + (PEEL1 + s)
                    split_lo(c + AHEAD, (PEEL1 + s + AHEAD) % RING)
                    in_tile(c, bank(PEEL1 + s), c)
            dve.wait_ge(consts_landed, ALL_CONSTS)
            lam_in = col[0:64, C_LAM:C_LAM + 4].rearrange("p (a b) -> p a b", a=2)
            dve.tensor_tensor(small[0:64, 38:40].unsqueeze(2), lam_in[:, :, 0:1], lam_in[:, :, 1:2], ALU.mult)\
               .then_inc(lam_products, 1)
            b = aux_bank()
            dve.tensor_scalar(S_f[0:16, 0:SEQ], PS[0:16, b, 0:SEQ], 1.0 / HD, EPS, ALU.mult, ALU.add).then_inc(aux_free, ax.up())
            inverse_root(S_f[0:16, 0:SEQ], S_f[0:16, 256:512], head_root, 1)
            dve.wait_ge(out_free, IN1)
            for i in range(2):
                dve.wait_ge(conv_gate, i + 1)
                step(dve.tensor_tensor(U[:, i, CONVW - 1:], qk[:, i, 0:SEQ], qk[:, 2 + i, 0:SEQ], ALU.mult))
            for t in range(8):
                b = aux_bank()
                g = C_QN1 + t // 4
                dve.scalar_tensor_tensor(qk[:, 6 + t, 0:SEQ], qk[:, 6 + t, 0:SEQ], col[:, g:g + 1], PS[:, b, 0:SEQ],
                                         ALU.mult, ALU.mult).then_inc(aux_free, ax.up())
            b = aux_bank()
            dve.tensor_copy(small[:, 40:42], PS[:, b, 0:2]).then_inc(aux_free, ax.up())
            for k in range(CONVW):
                for i in range(2):
                    w = col[:, C_CONVW + 2 * k + i:C_CONVW + 2 * k + i + 1]
                    u = U[:, i, k:k + SEQ]
                    if k == 0:
                        ins = dve.tensor_scalar(Y[:, i, :], u, w, col[:, C_CONVB + i:C_CONVB + i + 1], ALU.mult, ALU.add)
                    else:
                        dve.wait_ge(dve_step, st.now - (1 - i if k == CONVW - 1 else 1))
                        ins = dve.scalar_tensor_tensor(Y[:, i, :], u, w, Y[:, i, :], ALU.mult, ALU.add)
                    if k < CONVW - 1:
                        ins.then_inc(dve_step, st.up())
                    else:
                        ins.then_inc(conv_done, 1)
            dve.wait_ge(conv_done, 2)
            b = aux_bank()
            for i in range(2):
                ins = dve.scalar_tensor_tensor(YC[:, i, :], PS[:, b, 0:SEQ], -1.0 / 256, Y[:, i, :], ALU.mult, ALU.add)
                if i == 0:
                    ins.then_inc(conv_centred, 1)
                else:
                    ins.then_inc(aux_free, ax.up())
            b = aux_bank()
            dve.tensor_scalar(S_f[:, 512:768], PS[:, b, 0:SEQ], 1.0 / 256, EPS, ALU.mult, ALU.add).then_inc(aux_free, ax.up())
            inverse_root(S_f[:, 512:768], S_f[:, 768:1024], conv_root, 1)
            dve.wait_ge(conv_root, 1)
            for i in range(2):
                dve.tensor_tensor(YC[:, i, :], YC[:, i, :], S_f[:, 768:1024], ALU.mult).then_inc(conv_scaled, 1)
            for i in range(2):
                dve.wait_ge(mix1_hi, i + 1)
                b = aux_bank()
                dve.scalar_tensor_tensor(a_lo[:, i, 0:SEQ], PS[:, b, 0:SEQ], col[:, C_PWB + i:C_PWB + i + 1],
                                         a_hi[:, i, 0:SEQ].bitcast(F32), ALU.add, ALU.subtract).then_inc(aux_free, ax.up())
            for i in range(2):
                dve.wait_ge(mix1_hi, 2 + i + 1)
                b = aux_bank()
                dve.scalar_tensor_tensor(a_lo[:, 2 + i, 0:SEQ], PS[:, b, 0:SEQ], col[:, C_PS + i:C_PS + i + 1],
                                         a_hi[:, 2 + i, 0:SEQ].bitcast(F32), ALU.mult, ALU.subtract).then_inc(aux_free, ax.up())
            for t in range(HEADS1):
                b = aux_bank()
                dve.tensor_copy(v_tok[:, 0:2, t * P:(t + 1) * P],
                                PS[:, b, 0:2 * P].rearrange("p (k c) -> p k c", k=2)).then_inc(aux_free, ax.up())
            dve.wait_ge(lam_exp, 1)
            step(dve.tensor_tensor(small[:, 47:48], small[:, 42:43], small[:, 43:44], ALU.subtract))
            step(dve.tensor_scalar(small[:, 47:48], small[:, 47:48], LAM_INIT, None, ALU.add))
            for hd in range(HEADS1):
                for m in range(2):
                    b = aux_bank()
                    for qt in range(2):
                        k, e = (qt + 1) * P, 2 * m + qt
                        ins = dve.tensor_tensor_reduce(B1S(m, qt, k), PS[:, b, qt * P:qt * P + k], alibi[:, hd, qt, 0:k],
                                                       -0.125, 3.0e38, ALU.add, ALU.min, small[:, 48 + e:49 + e])
                        if qt == 0:
                            ins.then_inc(logits1_ready, 1)
                        else:
                            ins.then_inc(aux_free, ax.up())
                dve.wait_ge(exp1_done, 4 * (hd + 1))
                step(dve.reciprocal(small[:, 56:60], small[:, 52:56]))
                step(dve.tensor_scalar(small[:, 58:60], small[:, 58:60], small[:, 47:48], None, ALU.mult))
                for qt in range(2):
                    k = (qt + 1) * P
                    step(dve.tensor_scalar(B1S(1, qt, k), B1S(1, qt, k), small[:, 58 + qt:59 + qt], None, ALU.mult))
                    dve.scalar_tensor_tensor(B1S(0, qt, k), B1S(0, qt, k), small[:, 56 + qt:57 + qt], B1S(1, qt, k),
                                             ALU.mult, ALU.subtract).then_inc(probs1_mixed, 1)
                b = aux_bank()
                dve.tensor_copy(PTf[:, 0:3 * P], PS[:, b, 0:3 * P]).then_inc(aux_free, ax.up())
                b = aux_bank()
                dve.tensor_copy(qk[:, hd, 0:SEQ], PS[:, b, 0:SEQ]).then_inc(aux_free, ax.up())
            keep = (1.0 - LAM_INIT) ** 2
            b = aux_bank()
            dve.tensor_scalar(S_f[0:4, 0:SEQ], PS[0:4, b, 0:SEQ], 1.0 / (P * keep), EPS / keep, ALU.mult, ALU.add)\
               .then_inc(aux_free, ax.up())
            inverse_root(S_f[0:4, 0:SEQ], S_f[0:4, 256:512], o_root, 1)
            for t in range(HEADS1):
                b = aux_bank()
                dve.scalar_tensor_tensor(qk[:, t, 0:SEQ], qk[:, t, 0:SEQ], col[:, C_SUB:C_SUB + 1], PS[:, b, 0:SEQ],
                                         ALU.mult, ALU.mult).then_inc(aux_free, ax.up())
            for t in range(HEADS1):
                dve.wait_ge(mix1_hi, 4 + t + 1)
                dve.wait_ge(aux_free, B1E["o_cast", t] + 1)
                dve.tensor_tensor(a_lo[:, 4 + t, 0:SEQ], qk[:, t, 0:SEQ], a_hi[:, 4 + t, 0:SEQ].bitcast(F32),
                                  ALU.subtract).then_inc(mix1_lo, 1)
            for c in range(OUT1):
                n = IN1 + c
                split_lo(n + AHEAD, (n + AHEAD) % RING)
                dve.wait_ge(chunk_used, n + 1)
                dve.scalar_tensor_tensor(h[:, c, 0:SEQ], PS[:, bank(n), 0:SEQ], 1.0, h[:, c, 0:SEQ],
                                         ALU.mult, ALU.add).then_inc(out_free, 1)
                dve.wait_ge(out_free, n + 1)
                step(dve.tensor_scalar(qk[:, 8 + c, 0:SEQ], h[:, c, 0:SEQ], col[:, C_G + KD + c:C_G + KD + c + 1], None, ALU.mult))
                norm_lo(1, c)
            mean_square(1)
            b = aux_bank()
            dve.tensor_tensor(S_f[0:20, 0:SEQ], PS[0:20, b, 0:SEQ], rstd[0:20, 0:SEQ], ALU.mult).then_inc(aux_free, ax.up())
            dve.wait_ge(aux_free, ax.now)
            dve.tensor_scalar(S_f[0:20, 0:SEQ], S_f[0:20, 0:SEQ], col[0:20, C_RB:C_RB + 1], None, ALU.add)\
               .then_inc(router_logits, 1)
            b = aux_bank()
            LG = S_f[:, 512:552]
            dve.tensor_copy(LG, PS[:, b, 0:40]).then_inc(aux_free, ax.up())
            dve.wait_ge(aux_free, ax.now)
            LG3 = LG.rearrange("p (t x) -> p t x", t=2)
            first_of = S_f[:, 640:644]
            for i in range(4):
                step(dve.memset(S_f[:, 640 + i:641 + i], float(4 - i)))

            def first_max(src, top, onehot):
                step(dve.tensor_reduce(top, src, AX.X, ALU.max))
                step(dve.tensor_tensor(onehot, src, top.unsqueeze(2).to_broadcast([P, 2, 4]), ALU.is_equal))
                step(dve.tensor_tensor(onehot, onehot, first_of.unsqueeze(1).to_broadcast([P, 2, 4]), ALU.mult))
                step(dve.tensor_reduce(S_f[:, 644:646], onehot, AX.X, ALU.max))
                step(dve.tensor_tensor(onehot, onehot, S_f[:, 644:646].unsqueeze(2).to_broadcast([P, 2, 4]), ALU.is_equal))

            def v24(off):
                return S_f[:, off:off + 8].rearrange("p (t x) -> p t x", t=2)

            mg, og, le, o1, o2 = S_f[:, 646:648], v24(648), v24(656), v24(664), v24(672)
            m1, m2, gp, den = S_f[:, 680:682], S_f[:, 682:684], S_f[:, 684:686], S_f[:, 686:688]
            grp = LG3[:, :, 0:4]
            first_max(grp, mg, og)
            dve.tensor_tensor(small_g().rearrange("p (t x) -> p t x", t=2), grp, mg.unsqueeze(2).to_broadcast([P, 2, 4]),
                              ALU.subtract).then_inc(router_centred, 1)
            t4 = S_f[:, 700:732].rearrange("p (t e g) -> p t e g", t=2, e=4)
            for t in range(2):
                step(dve.tensor_tensor(t4[:, t], LG3[:, t, 4:20].rearrange("p (g e) -> p e g", g=4),
                                       og[:, t].unsqueeze(1).to_broadcast([P, 4, 4]), ALU.mult))
            step(dve.tensor_reduce(le, t4, AX.X, ALU.add))
            first_max(le, m1, o1)
            t24 = v24(732)
            step(dve.scalar_tensor_tensor(t24, o1, -1.0e30, le, ALU.mult, ALU.add))
            first_max(t24, m2, o2)
            dve.tensor_tensor(small[:, 90:92], m2, m1, ALU.subtract).then_inc(router_centred, 1)
            dve.wait_ge(router_exp, 1)
            step(dve.tensor_reduce(gp, small_g().rearrange("p (t x) -> p t x", t=2), AX.X, ALU.add))
            dve.wait_ge(router_exp, 2)
            step(dve.tensor_scalar(den, small[:, 90:92], 1.0, None, ALU.add))
            step(dve.tensor_tensor(den, den, gp, ALU.mult))
            step(dve.reciprocal(den, den))
            step(dve.tensor_tensor(gp, den, small[:, 90:92], ALU.mult))
            step(dve.tensor_tensor(o1, o1, den.unsqueeze(2).to_broadcast([P, 2, 4]), ALU.mult))
            step(dve.tensor_tensor(o2, o2, gp.unsqueeze(2).to_broadcast([P, 2, 4]), ALU.mult))
            step(dve.tensor_tensor(o1, o1, o2, ALU.add))
            for t in range(2):
                gt = S_f[:, 600 + 16 * t:616 + 16 * t].rearrange("p (g e) -> p g e", g=4)
                dve.tensor_tensor(gt, o1[:, t].unsqueeze(1).to_broadcast([P, 4, 4]),
                                  og[:, t].unsqueeze(2).to_broadcast([P, 4, 4]), ALU.mult).then_inc(gates_ready, 1)
            b = aux_bank()
            dve.tensor_copy(S_f[0:16, 256:512], PS[0:16, b, 0:SEQ]).then_inc(aux_free, ax.up())
            for e in range(8):
                b = aux_bank()
                dve.tensor_tensor(gates_bc[:, 2 * e:2 * e + 2, :], PS[:, b, 0:512].rearrange("p (u t) -> p u t", u=2),
                                  rstd[:, 0:SEQ].unsqueeze(1).to_broadcast([P, 2, SEQ]), ALU.mult).then_inc(aux_free, ax.up())
            dve.wait_ge(aux_free, ax.now)
            assert ax.n == B1_AUX
            cb, ob = IN1 + OUT1, IN1 + OUT1
            for half in range(2):
                ffn_up(cb, cb % RING, ob, bank(ob), MOE_HALF, SEQ, None, half * 8)
                down(cb + 2 * MOE_HALF, (cb + 2 * MOE_HALF) % RING, ob + 2 * MOE_HALF, bank(ob + 2 * MOE_HALF),
                     MOE_HALF, 1.0, 2 if half else None, SEQ)
                cb += MOE_C
                ob += 2 * MOE_HALF + KD
            dve.memset(biasB[:, :, :, SEQ:L], 0.0).then_inc(setup_done, 1)

            with dve.Fori(0, LAYERS) as l:
                ax.enter(l, LAYER_A)
                st.enter(l, DVE_STEPS)
                cb = l * LAYER_C + B1_CHUNKS
                ob = l * LAYER_O + B1_OUTS
                sl, bk = B2S, B2B
                ff.enter(l, 2 * FT)
                ffn_up(cb, sl, ob, bk, FT, L, l * 3 + 2)
                down(cb + FFN_UP, (sl + FFN_UP) % RING, ob + FFN_UP, (bk + FFN_UP) % 4, FT, 0.5, l * 3 + 3, L)
                c, o = FFN_C, FFN_UP + KD
                roped_before = 0
                for t, (kind, i) in enumerate(QKV_ORDER):
                    split_lo(cb + (c + t + AHEAD), (sl + c + t + AHEAD) % RING)
                    if t == 0:
                        mean_square(l * 3 + 3)
                    dve.wait_ge(chunk_used, cb + (c + t + 1))
                    ps = PS[:, (bk + o + t) % 4, 0:L]
                    dst = vstage[i % 2] if kind == "v" else qk[:, R_OF[kind] + i, :]
                    if kind == "qB":
                        dve.scalar_tensor_tensor(dst, ps, 0.125, rstd[:, :], ALU.mult, ALU.mult).then_inc(out_free, 1)
                    else:
                        dve.tensor_tensor(dst, ps, rstd[:, :], ALU.mult).then_inc(out_free, 1)
                    for what, i in QKV_EVENTS.get(t, []):
                        if what == "stat":
                            continue
                        b = aux_bank()
                        if what in ("swapA", "swapC"):
                            tab = M_TAB + (0 if what == "swapA" else 2 * L)
                            if what == "swapC":
                                dve.wait_ge(aux_free, ax.now)
                            rot = S_sb[:, 1, 0, :]
                            if roped_before:
                                dve.wait_ge(roped, l * 10 + roped_before)
                            roped_before += 1
                            dve.tensor_tensor(rot, PS[:, b, 0:L], mat[:, tab + L:tab + 2 * L], ALU.mult).then_inc(aux_free, ax.up())
                            step(dve.tensor_tensor(qk[:, i, :], qk[:, i, :], mat[:, tab:tab + L], ALU.mult))
                            dve.wait_ge(aux_free, ax.now)
                            dve.tensor_tensor(qk[:, i, :], qk[:, i, :], rot, ALU.add).then_inc(roped, 1)
                        elif what == "v":
                            step(dve.tensor_copy(v_tok[:, 0:2, i * P:(i + 1) * P],
                                                 PS[:, b, 0:2 * P].rearrange("p (k c) -> p k c", k=2)))
                            dve.tensor_copy(v_tok[0:META, 2, i * P:(i + 1) * P], PS[0:META, b, 2 * P:3 * P])\
                               .then_inc(aux_free, ax.up())
                        elif what == "sumC":
                            dve.tensor_scalar(G[0:10, 8, :], PS[0:10, b, 0:L], 1.0 / HD, EPS, ALU.mult, ALU.add)\
                               .then_inc(aux_free, ax.up())
                            inverse_root(G[0:10, 8, :], G[0:10, 9, :], c_rstd, 1)
                        else:
                            r = C_TILES[i]
                            gn = bass.ds(l * 2 + C_QN + (1 if i == 0 else 0), 1)
                            dve.scalar_tensor_tensor(qk[:, r, :], qk[:, r, :], col[:, gn], PS[:, b, 0:L],
                                                     ALU.mult, ALU.mult).then_inc(aux_free, ax.up())
                c, o = c + QKV_T, o + QKV_T
                nexp = Count()

                def turned(j):
                    dve.wait_ge(probsT_out, l * 24 + j + 1)
                    dve.tensor_copy(PT[:, 0, :], PS[:, 5, 0:L]).then_inc(probsT_dve, 1)
                    dve.tensor_copy(PT[0:META, 2, 0:P], PS[0:META, 5, L:L + P]).then_inc(probsT_dve, 1)
                    dve.tensor_copy(PT[0:META, 2, 2 * P:L], PS[0:META, 5, L + P:L + P + META]).then_inc(probsT_dve, 1)

                for j in range(24):
                    typ = j // 8
                    if typ == 1:
                        dve.wait_ge(bias_ready, l * 8 + (j - 8 + 1))
                    if j == 0:
                        step(dve.tensor_scalar(small[:, 68:76], col[:, bass.ds(l * 8 + C_SINK, 8)], -1.0, None, ALU.mult))
                    dve.wait_ge(scores_out, l * 72 + 3 * j + 3)
                    split_lo(cb + (c + j + AHEAD), (sl + c + j + AHEAD) % RING)
                    jj = 3 * (j % 2)
                    for qt in range(3):
                        r = q_rows(qt)
                        if typ == 0:
                            bias = mat[0:r, M_MA + qt * L:M_MA + (qt + 1) * L]
                            hA = j // 2 + 4 * (j % 2)
                            init = small[0:r, 68 + hA:69 + hA]
                        elif typ == 1:
                            bias = biasB[:, j % 2, qt, :] if qt < 2 else mat[0:r, M_MBM:M_MBM + L]
                            init = 3.0e38
                        else:
                            bias = zero[0:r, :].to_broadcast([r, L])
                            init = 3.0e38
                        dve.tensor_tensor_reduce(S_sb[0:r, j % 2, qt, :], PS[0:r, 2 + qt, 0:L], bias,
                                                 -1.0 if typ == 1 else -0.125, init, ALU.add, ALU.min,
                                                 minl[0:r, jj + qt:jj + qt + 1]).then_inc(logits_ready, 1)
                    if j > 0:
                        turned(j - 1)
                    nexp.up(4 if j < 8 else 3)
                    dve.wait_ge(exp_done, l * 80 + nexp.n)
                    total = rsum
                    if j < 8:
                        total = esink
                        step(dve.tensor_tensor(esink[:, jj:jj + 3], rsum[:, jj:jj + 3], esink[:, jj:jj + 3], ALU.add))
                    dve.reciprocal(rden[:, jj:jj + 3], total[:, jj:jj + 3]).then_inc(rden_ready, 1)
                    if j % 2 == 1 and j > 1:
                        pair_lo(dve, l, (j - 3) // 2)
                    dve.wait_ge(chunk_used, cb + (c + j + 1))
                    dve.tensor_tensor(G[:, j, :], PS[:, j % 2, 0:L], rstd[:, :], ALU.mult).then_inc(out_free, 1)
                turned(23)
                pair_lo(dve, l, 11)
                c, o = c + GATE_T, o + GATE_T
                for s in range(BRANCH_C):
                    split_lo(cb + (c + s + AHEAD), (sl + c + s + AHEAD) % RING)
                    dve.wait_ge(chunk_used, cb + (c + s + 1))
                    for u in (2 * s, 2 * s + 1):
                        n, m = u % 3, u // 3
                        dve.wait_ge(gate_sig, l * 24 + u + 1)
                        dve.tensor_tensor(S_sb[:, m % 2, n, :], PS[:, (bk + o + u) % 4, 0:L], G[:, n * KD + m, :],
                                          ALU.mult).then_inc(out_free, 1)
                        if n == 1:
                            dve.wait_ge(out_free, ob + (o + u + 1))
                            step(dve.tensor_tensor(S_sb[:, m % 2, 0, :], S_sb[:, m % 2, 0, :], S_sb[:, m % 2, 1, :], ALU.add))
                        if n == 2:
                            dve.wait_ge(out_free, ob + (o + u + 1))
                            dve.tensor_tensor(S_sb[:, m % 2, 0, :], S_sb[:, m % 2, 0, :], S_sb[:, m % 2, 2, :],
                                              ALU.add).then_inc(mixed_ready, 1)
                            dve.wait_ge(mix_hi_done, l * KD + m + 1)
                            dve.tensor_tensor(a_lo[:, 12 + m, :], S_sb[:, m % 2, 0, :], a_hi[:, 12 + m, :].bitcast(F32),
                                              ALU.subtract).then_inc(mix_lo_done, 1)
                c, o = c + BRANCH_C, o + 3 * KD
                for m in range(OUT_C):
                    split_lo(cb + (c + m + AHEAD), (sl + c + m + AHEAD) % RING)
                    dve.wait_ge(chunk_used, cb + (c + m + 1))
                    residual(l * 3 + 4, m, ob + (o + m), (bk + o + m) % 4, 1.0, L)
                c, o = c + OUT_C, o + KD
                ffn_up(cb + c, (sl + c) % RING, ob + o, (bk + o) % 4, FT, L, l * 3 + 4)
                down(cb + (c + FFN_UP), (sl + c + FFN_UP) % RING, ob + (o + FFN_UP), (bk + o + FFN_UP) % 4, FT, 0.5, l * 3 + 5, L)
                ff.leave(LAYERS)
                st.leave(LAYERS)
                ax.leave(LAYERS)
            mean_square(8)
            for m in range(KD):
                dve.scalar_tensor_tensor(qk[:, m, 0:SEQ], h[:, m, 0:SEQ], col[:, C_G + 8 * KD + m:C_G + 8 * KD + m + 1],
                                         rstd[:, 0:SEQ], ALU.mult, ALU.mult).then_inc(out_ready, 1)

        @block.gpsimd
        def _(pool):
            st = Count()

            def step(ins):
                ins.then_inc(pool_step, st.up())
                pool.wait_ge(pool_step, st.now)

            def sum_squares(o, n0=0):
                for m in range(KD):
                    if o is not None:
                        pool.wait_ge(out_free, o + (m + 1))
                    if m == 0:
                        step(pool.tensor_tensor(acc, h[:, 0, :], h[:, 0, :], ALU.mult))
                        continue
                    step(pool.tensor_tensor(sq, h[:, m, :], h[:, m, :], ALU.mult))
                    ins = pool.tensor_tensor(acc, acc, sq, ALU.add)
                    if m < KD - 1:
                        step(ins)
                    else:
                        ins.then_inc(squares_summed, 1)

            pool.wait_ge(setup_done, 1)
            pool.wait_ge(inputs_landed, 32)
            sum_squares(None)
            pool.wait_ge(out_free, IN1)
            pool.wait_ge(consts_landed, ALL_CONSTS)
            step(pool.tensor_copy(UP[:, :, 16:272], qk[:, 4:6, 0:SEQ]))
            ladder = [UW, S_f[:, 1024:1568].rearrange("p (i t) -> p i t", i=2)]
            last, w = UP, 1
            for g in range(4):
                nxt, r0 = ladder[g % 2], 2 * w - 1
                step(pool.tensor_tensor(nxt[:, :, r0:272], last[:, :, r0:272], last[:, :, r0 - w:272 - w], ALU.add))
                t, p0 = g // 2, 64 * (g % 2)
                step(pool.tensor_tensor(qk[p0:p0 + 64, 4 + t, 0:SEQ], nxt[p0:p0 + 64, t, 16:272],
                                        invcount[p0:p0 + 64, t, :], ALU.mult))
                last, w = nxt, 2 * w
            pool.tensor_tensor(qk[:, 4:6, 0:SEQ], qk[:, 4:6, 0:SEQ], UP[:, :, 16:272], ALU.subtract).then_inc(pooled, 1)
            sum_squares(IN1)
            sum_squares(B1_OUTS - KD)

            with pool.Fori(0, LAYERS) as l:
                st.enter(l, POOL_STEPS)
                ob = l * LAYER_O + B1_OUTS
                sum_squares(ob + FFN_UP)
                for j in range(24):
                    pool.wait_ge(rden_ready, l * 24 + j + 1)
                    for qt in range(3):
                        r = q_rows(qt)
                        e = 3 * (j % 2) + qt
                        pool.tensor_tensor(S_sb[0:r, j % 2, qt, :], S_sb[0:r, j % 2, qt, :],
                                           rden[0:r, e:e + 1].to_broadcast([r, L]), ALU.mult).then_inc(probs_ready, 1)
                    if 7 <= j < 15:
                        hB = j - 7
                        pool.wait_ge(bias_landed[hB % 2], l * 256 + 64 * (hB // 2 + 1))
                        for qt in range(2):
                            ins = pool.tensor_tensor(biasB[:, hB % 2, qt, 0:SEQ], biasB[:, hB % 2, qt, 0:SEQ],
                                                     mat[:, M_MB + qt * SEQ:M_MB + (qt + 1) * SEQ], ALU.add)
                            if qt == 0:
                                step(ins)
                            else:
                                ins.then_inc(bias_ready, 1)
                sum_squares(ob + (FFN_UP + KD + QKV_T + GATE_T + 3 * KD))
                sum_squares(ob + (LAYER_O - KD))
                st.leave(LAYERS)


def dense_mask(allowed):
    return np.where(allowed, 0.0, -1.0e30).astype(np.float32)


def by_query_tile(a):
    n = -(-a.shape[0] // P)
    full = np.zeros((n * P, a.shape[1]), np.float32)
    full[:a.shape[0]] = a
    return full.reshape(n, P, -1).transpose(1, 0, 2).reshape(P, -1)


def constants():
    c = np.zeros((P, NM), np.float32)
    c[:, M_ID:M_ID + P] = np.eye(P)
    c[:, M_ONES:M_ONES + P] = 1.0
    p = np.arange(P)
    c[(p + 32) % 64 + p // 64 * 64, M_PA + p] = 1.0
    c[(p + 16) % 32 + p // 32 * 32, M_PC + p] = 1.0
    for t in range(8):
        c[p, M_SEL16 + 16 * t + 2 * t + p // 64] = 1.0
    for t in range(4):
        c[:, M_SEL4 + 4 * t + t] = 1.0
    pos = np.concatenate([np.arange(SEQ) + META, np.arange(META)])
    t = pos - META
    row = np.where(t >= 0, t // 64, -1).astype(np.float32)
    column = np.where(t >= 0, t % 64, pos).astype(np.float32)

    def table(dim, where):
        inv = np.float32(10000.0) ** (-np.arange(0, dim, 2, dtype=np.float32) / np.float32(dim))
        ang = (where.astype(np.float32)[None, :] * inv[:, None]).astype(np.float32)
        cos, sin = np.cos(ang), np.sin(ang)
        return np.concatenate([cos, cos]), np.concatenate([-sin, sin])

    cosA, sinA = table(64, pos)
    (cr, sr), (cc, sc) = table(32, row), table(32, column)
    for k, a in enumerate((cosA, sinA, np.concatenate([cr, cc]), np.concatenate([sr, sc]))):
        c[:, M_TAB + k * L:M_TAB + (k + 1) * L] = np.concatenate([a, a])
    real = t >= 0
    band = (np.abs(pos[:, None] - pos[None, :]) <= 128) | ~real[None, :]
    c[:, M_MA:M_MA + 3 * L] = by_query_tile(dense_mask(band))
    c[:META, M_MBM:M_MBM + L] = dense_mask(np.broadcast_to(~real[None, :], (META, L)))
    qc = np.arange(SEQ) % 64
    start = np.clip(qc - 8, 0, 64 - 16)
    kc = qc[None, :]
    ok = (kc >= start[:, None]) & (kc < start[:, None] + 16)
    c[:, M_MB:M_MB + 2 * SEQ] = by_query_tile(dense_mask(ok))
    return c


def block1_constants():
    c = np.zeros((P, 2048 + 512), np.float32)
    tq = np.arange(SEQ)
    dist = (tq[:, None] - tq[None, :]).astype(np.float32)
    start = 2.0 ** (-8.0 / HEADS1)
    for hd in range(HEADS1):
        bias = np.where(dist >= 0, -np.float32(start ** (hd + 1)) * dist * 8, -1.0e30)
        c[:, hd * 512:(hd + 1) * 512] = by_query_tile(bias)
    for g, win in enumerate((2, 4, 8, 16)):
        inv = 1.0 / np.minimum(tq + 1, win).astype(np.float32)
        c[64 * (g % 2):64 * (g % 2) + 64, 2048 + SEQ * (g // 2):2048 + SEQ * (g // 2 + 1)] = inv
    return c


def tiles(w):
    K, N = w.shape
    return w.reshape(K // P, P, N // P, P).transpose(2, 0, 1, 3)


def kernel(**inputs):
    import concourse.bacc as bacc
    from concourse.bass_utils import run_bass_kernel_spmd

    a = {k: np.asarray(v) for k, v in inputs.items()}
    f = np.float32

    stream = np.empty((STREAM, P, BLK, P), f)
    at = 0

    def put(blocks):
        nonlocal at
        n = blocks.shape[0] // BLK
        stream[at:at + n] = blocks.reshape(n, BLK, P, P).transpose(0, 2, 1, 3)
        at += n

    def put_w(w):
        put(tiles(w).reshape(-1, P, P))

    w = a["w_in"][0]
    put_w(w)
    put_w(a["w_out"][0])
    for half in range(2):
        es = range(8 * half, 8 * half + 8)
        for e in es:
            g, u = tiles(a["w_gate"][0, e]), tiles(a["w_up"][0, e])
            put(np.stack([g, u], 1).reshape(-1, P, P))
        put_w(a["w_down"][0, 8 * half:8 * half + 8].reshape(-1, D))

    def ffn(w_in, w_out):
        g, u = tiles(w_in[:, :FF]), tiles(w_in[:, FF:])
        put(np.stack([g, u], 1).reshape(-1, P, P))
        put_w(w_out)

    pairs = np.concatenate([np.r_[64 * t:64 * t + 64, 64 * (t + 4):64 * (t + 4) + 64] for t in range(4)])
    for l in range(LAYERS):
        ffn(a["ffn1_w_in_2"][l], a["ffn1_w_out_2"][l])
        w = a["w_in_2"][l]
        qa, ka, va, qb, kb, vb, qc, kc, vc, gates = np.split(w, np.cumsum([512, 128, 128, 512, 512, 512, 512, 128, 128]), axis=1)
        for part in (ka, kc, kb, va, vc, vb, qa[:, pairs], qc[:, pairs], qb, gates):
            put_w(part)
        wb = [a["w_branch_2"][l, 0][pairs], a["w_branch_2"][l, 1], a["w_branch_2"][l, 2][pairs]]
        put(np.stack([tiles(x) for x in wb], 1).reshape(-1, P, P))
        put_w(a["w_out_2"][l])
        ffn(a["ffn2_w_in_2"][l], a["ffn2_w_out_2"][l])
    assert at == CHUNKS
    stream[at:] = stream[:STREAM - at]

    col = np.zeros((P, NC), f)

    def by_tile(v):
        return v.reshape(-1, P).T

    gains = [a["attn_norm_g"][0], a["ffn_norm_g"][0]]
    for l in range(LAYERS):
        gains += [a["ffn1_norm_2"][l], a["mix_norm_2"][l], a["ffn2_norm_2"][l]]
    gains.append(a["final_norm_2"])
    for v, g in enumerate(gains):
        col[:, C_G + v * KD:C_G + (v + 1) * KD] = by_tile(g)
    for l in range(LAYERS):
        col[:, C_QN + 2 * l] = np.tile(a["qnorm_c_2"][l], 2)
        col[:, C_QN + 2 * l + 1] = np.tile(a["knorm_c_2"][l], 2)
        col[:, C_SINK + 8 * l:C_SINK + 8 * l + 8] = a["sink_a_2"][l][None, :]
    for k in range(CONVW):
        col[:, C_CONVW + 2 * k:C_CONVW + 2 * k + 2] = by_tile(a["conv_w"][0, k])
    for at_, name in ((C_CONVB, "conv_b"), (C_LNG, "conv_ln_g"), (C_LNB, "conv_ln_b"), (C_PWB, "conv_pw_b"), (C_PS, "pool_scale")):
        col[:, at_:at_ + 2] = by_tile(a[name][0])
    col[:, C_QN1] = np.tile(a["q_norm_g"][0], 2)
    col[:, C_QN1 + 1] = np.tile(a["k_norm_g"][0], 2)
    col[:, C_SUB] = a["attn_sub_norm_g"][0]
    for k, name in enumerate(("lambda_q1", "lambda_k1", "lambda_q2", "lambda_k2")):
        col[:64, C_LAM + k] = a[name][0]
    col[:20, C_RB] = np.concatenate([a["router_g_b"][0], a["router_e_b"][0]])
    rw = np.concatenate([a["router_g_w"][0], a["router_e_w"][0]], axis=1)
    col[:, C_RW:] = rw.reshape(KD, P, 20).transpose(1, 0, 2).reshape(P, -1)

    b1 = np.zeros((P, 2048 + 512 + 512 + 256), f)
    b1[:, :2560] = block1_constants()
    b1[:, 2560:3072] = a["conv_pw_w"][0].reshape(2, P, 256).transpose(1, 0, 2).reshape(P, -1)
    for g in range(4):
        p0 = 64 * (g % 2)
        b1[p0:p0 + 64, 3072 + P * (g // 2) + p0:3072 + P * (g // 2) + p0 + 64] = a["pool_w"][0, g]

    rpb = np.zeros((LAYERS, 8, 7, 64, 128), f)
    rpb[:, :, :, :, 48:79] = a["rpb_b_2"][:, :, 4:11, None, :]

    x = np.concatenate([a["x"][0], a["meta_tokens_2"]], axis=0)
    xT = x.T.reshape(KD, P, L).transpose(1, 0, 2)

    arrays = {
        "stream": stream.reshape(STREAM, P, BLK * P), "xT": xT, "cols": col, "mats": constants(), "b1mats": b1, "rpbz": rpb,
    }
    arrays = {k: np.ascontiguousarray(v) for k, v in arrays.items()}
    nc = bacc.Bacc("TRN2", target_bir_lowering=False, num_devices=1)
    args = [nc.dram_tensor(k, v.shape, F32, kind="ExternalInput").ap() for k, v in arrays.items()]
    out = nc.dram_tensor("out", (P, KD, SEQ), F32, kind="ExternalOutput").ap()
    build(nc, *args, out)
    got = run_bass_kernel_spmd(nc, [arrays], core_ids=[0]).results[0]["out"]
    return np.ascontiguousarray(got.transpose(2, 1, 0).reshape(1, SEQ, D))
```

```python
from contextlib import ExitStack

import numpy as np

import concourse.bass as bass
from concourse import mybir

F32 = mybir.dt.float32
F32R = mybir.dt.float32r
I32 = mybir.dt.int32
ALU = mybir.AluOpType
ACT = mybir.ActivationFunctionType
AX = mybir.AxisListType

P = 128
D = 1024
KD = D // P
SEQ = 256
META = 16
L = SEQ + META
EPS = 1e-6
LAYERS = 2
HD = 64
FF = 2816
FT = FF // P
HEADS1 = 4
MOE_T = 4096 // P
MOE_HALF = MOE_T // 2
CONVW = 31
LAM_INIT = 0.2

BLK = 8
RING = 4
AHEAD = 3
IN1, OUT1 = 18, 8
PEEL1 = 6
MOE_C = 2 * MOE_HALF + MOE_HALF * KD // BLK
B1_CHUNKS = IN1 + OUT1 + 2 * MOE_C
FFN_UP, FFN_DOWN = 2 * FT, FT * KD // BLK
FFN_C = FFN_UP + FFN_DOWN
QKV_T, GATE_T = 24, 24
BRANCH_C, OUT_C = 3 * 4 * KD // BLK, KD
LAYER_C = 2 * FFN_C + QKV_T + GATE_T + BRANCH_C + OUT_C
CHUNKS = B1_CHUNKS + LAYERS * LAYER_C
STREAM = CHUNKS + AHEAD

B1_OUTS = IN1 + OUT1 + 2 * (2 * MOE_HALF + KD)
LAYER_O = 2 * (FFN_UP + KD) + QKV_T + GATE_T + 3 * KD + KD

R_KA, R_KC, R_KB, R_QA, R_QC, R_QB = 0, 1, 2, 6, 10, 14
QKV_ORDER = ([("kA", 0), ("kC", 0)] + [("kB", t) for t in range(4)] + [("v", t) for t in range(6)]
             + [("qC", t) for t in range(4)] + [("qA", t) for t in range(4)] + [("qB", t) for t in range(4)])
R_OF = {"kA": R_KA, "kC": R_KC, "kB": R_KB, "qA": R_QA, "qC": R_QC, "qB": R_QB}
C_TILES = [R_KC] + [R_QC + t for t in range(4)]
QKV_EVENTS = {0: [("stat", 0)], 4: [("swapA", R_KA)], 16: [("sumC", 0)]}
for _t in range(6):
    QKV_EVENTS[7 + _t] = [("v", _t)]
for _t in range(4):
    QKV_EVENTS[17 + _t] = [("swapA", R_QA + _t)]
QKV_EVENTS[20] += [("castC", i) for i in range(5)]
QKV_EVENTS[22] = [("swapC", r) for r in C_TILES]
QKV_EVENT_LIST = [e for t in range(QKV_T) for e in QKV_EVENTS.get(t, [])]
AUX_QKV = len(QKV_EVENT_LIST)
LAYER_A = 2 + AUX_QKV
CASTC_IN_LAYER = 1 + QKV_EVENT_LIST.index(("castC", 0))
B1_EVENTS = ([("stat", 0), ("conv_mean", 0), ("qk_sum", 0), ("lambda", 0)] + [("qk_cast", t) for t in range(8)]
             + [("score0", 0), ("score1", 0)] + [("v", t) for t in range(HEADS1)] + [("conv_cast", 0)]
             + [("score0", 1), ("score1", 1)]
             + [e for t in range(HEADS1) for e in
                [("turn", t)] + ([("score0", t + 2), ("score1", t + 2)] if t + 2 < HEADS1 else []) + [("pv", t)]]
             + [("o_sum", 0)] + [("pointwise", i) for i in range(2)] + [("pool", i) for i in range(2)]
             + [("o_cast", t) for t in range(HEADS1)]
             + [("stat", 1), ("router", 0), ("router_turn", 0), ("gates_turn", 0)]
             + [("gates_cast", e) for e in range(8)])
B1E = {e: i for i, e in enumerate(B1_EVENTS)}
B1_AUX = len(B1_EVENTS)
DVE_STEPS = 55

POOL_STEPS = 68

SKEW = 64 * 128

C_G = 0
C_QN = C_G + 9 * KD
C_SINK = C_QN + 2 * LAYERS
C_CONVW = C_SINK + 8 * LAYERS
C_CONVB = C_CONVW + 2 * CONVW
C_LNG, C_LNB, C_PWB = C_CONVB + 2, C_CONVB + 4, C_CONVB + 6
C_PS = C_PWB + 2
C_QN1 = C_PS + 2
C_SUB = C_QN1 + 2
C_LAM = C_SUB + 1
C_RB = C_LAM + 4
C_RW = C_RB + 1
NC = C_RW + KD * 20
M_ID, M_ONES, M_PA, M_PC = 0, P, 2 * P, 3 * P
M_SEL16 = 4 * P
M_SEL4 = M_SEL16 + 9 * 17
M_TAB = M_SEL4 + 16
M_MA = M_TAB + 4 * L
M_MBM = M_MA + 3 * L
M_MB = M_MBM + L
NM = M_MB + 2 * SEQ


class Count:

    def __init__(self, start=0):
        self.n, self.term, self.stack = start, 0, []

    def up(self, k=1):
        self.n += k
        return k

    @property
    def now(self):
        return self.term + self.n

    def enter(self, i, per, first=0):
        self.stack.append((self.n, self.term, per, first))
        self.term = self.term + i * per
        self.n -= first * per

    def leave(self, turns):
        n0, term, per, first = self.stack.pop()
        assert self.n - (n0 - first * per) == per, (self.n - (n0 - first * per), per)
        self.term, self.n = term, n0 + per * turns


def build(nc, stream, xT, cols, mats, b1mats, spread, rpbz, out):
    with ExitStack() as ctx:
        def sb(name, shape, dt=F32):
            return ctx.enter_context(nc.sbuf_tensor(name, shape, dt))

        def sem(name):
            return ctx.enter_context(nc.semaphore(name))

        raw = sb("raw", [P, RING, BLK * P])
        w_hi = sb("w_hi", [P, RING, BLK * P], F32R)
        w_lo = sb("w_lo", [P, RING, BLK * P], F32R)
        h = sb("h", [P, KD, L])
        x_hi = sb("x_hi", [P, KD, L], F32R)
        x_lo = sb("x_lo", [P, KD, L], F32R)
        a_hi = sb("a_hi", [P, FT, L], F32R)
        a_lo = sb("a_lo", [P, FT, L], F32R)
        qk = sb("qk", [P, 18, L])
        G = sb("G", [P, GATE_T, L])
        v_tok = sb("v_tok", [P, 3, 6 * P])
        S_sb = sb("S_sb", [P, 2, 3, L])
        PT = sb("PT", [P, 3, L])
        biasB = sb("biasB", [P, 2, 2, L])
        rstd = sb("rstd", [P, L])
        col = sb("col", [P, NC])
        mat = sb("mat", [P, NM])
        small = sb("small", [P, 96])
        PS = ctx.enter_context(nc.psum_tensor("PS", [P, 8, 512], F32))

        ident, ones = mat[:, M_ID:M_ID + P], mat[:, M_ONES:M_ONES + P]
        Gf = G[:, :, :].rearrange("p a b -> p (a b)")
        vstage = [G[:, 6, :], G[:, 7, :]]
        acc, sq, ms = G[:, 20, :], G[:, 21, :], G[:, 22, :]
        half_acc = G[:, 17, :]
        tap_products = [sq, ms, G[:, 23, :]]
        zero = small[:, 1:2]
        minl, rsum, rden, esink = (small[:, 4 + 8 * i:4 + 8 * i + 6] for i in range(4))
        alibi = Gf[:, 0:2048].rearrange("p (h t k) -> p h t k", h=4, t=2)
        U = Gf[:, 2048:2620].rearrange("p (i t) -> p i t", i=2)
        Y = Gf[:, 2624:3136].rearrange("p (i t) -> p i t", i=2)
        YC = Gf[:, 3136:3648].rearrange("p (i t) -> p i t", i=2)
        YS = Gf[:, 3648:4160].rearrange("p (i t) -> p i t", i=2)
        UP = Gf[:, 4160:4704].rearrange("p (i t) -> p i t", i=2)
        UW = Gf[:, 4704:5248].rearrange("p (i t) -> p i t", i=2)
        qk_f = qk[:, :, :].rearrange("p a b -> p (a b)")
        O2 = qk[:, 14:18, 0:SEQ]
        gates_T = qk[0:16, 16, 0:SEQ]
        spread_sb = qk_f[0:16, 0:8 * P]
        PTf = PT[:, :, :].rearrange("p a b -> p (a b)")
        pool_w = PTf[:, 384:640].rearrange("p (i c) -> p i c", i=2)
        bB = biasB[:, :, :, :].rearrange("p a b c -> p (a b c)")
        invcount = bB[:, 0:512].rearrange("p (i t) -> p i t", i=2)
        pw_w = bB[:, 512:1024].rearrange("p (k c) -> p k c", k=2)
        S_f = S_sb[:, :, :, :].rearrange("p a b c -> p (a b c)")
        v_f = v_tok[:, :, :].rearrange("p a b -> p (a b)")
        head_ms, head_rs = S_f[0:17, 0:SEQ], v_f[0:17, 8 * SEQ:9 * SEQ]
        gates_bc = Gf[:, 0:16 * SEQ].rearrange("p (e t) -> p e t", e=16)

        raw_landed = [sem(f"raw_landed{s}") for s in range(RING)]
        hi_done, lo_done = sem("hi_done"), sem("lo_done")
        chunk_used = sem("chunk_used")
        out_free = sem("out_free")
        aux_out, aux_free = sem("aux_out"), sem("aux_free")
        inputs_landed, consts_landed = sem("inputs_landed"), sem("consts_landed")
        x_hi_done, x_lo_done = sem("x_hi_done"), sem("x_lo_done")
        squares_summed, rstd_done = sem("squares_summed"), sem("rstd_done")
        act_done, a_ready = sem("act_done"), sem("a_ready")
        a_hi_done, a_lo_done = sem("a_hi_done"), sem("a_lo_done")
        c_squared, c_rstd, roped = sem("c_squared"), sem("c_rstd"), sem("roped")
        scores_out, logits_ready, exp_done, rden_ready = (
            sem("scores_out"), sem("logits_ready"), sem("exp_done"), sem("rden_ready"))
        probs_ready, probsT_out, probsT_dve, probsT_act = (
            sem("probs_ready"), sem("probsT_out"), sem("probsT_dve"), sem("probsT_act"))
        pv_out, o_hi_done, o_lo_done = sem("pv_out"), sem("o_hi_done"), sem("o_lo_done")
        bias_landed = [sem(f"bias_landed{i}") for i in range(2)]
        bias_ready = sem("bias_ready")
        gate_sig, mixed_ready, mix_hi_done, mix_lo_done = (
            sem("gate_sig"), sem("mixed_ready"), sem("mix_hi_done"), sem("mix_lo_done"))
        setup_done, spread_landed = sem("setup_done"), sem("spread_landed")
        conv_input, conv1_done = sem("conv_input"), sem("conv1_done")
        half_summed, ones_landed = sem("half_summed"), sem("ones_landed")
        tap_product, tap_added = sem("tap_product"), sem("tap_added")
        dve_step, pool_step = sem("dve_step"), sem("pool_step")
        conv_gate, qk_squared, lam_exp = sem("conv_gate"), sem("qk_squared"), sem("lam_exp")
        conv_squared, conv_act, mix1_hi = sem("conv_squared"), sem("conv_act"), sem("mix1_hi")
        exp1_done, o_squared, router_exp = sem("exp1_done"), sem("o_squared"), sem("router_exp")
        lam_products, conv_done, conv_centred, conv_scaled = (
            sem("lam_products"), sem("conv_done"), sem("conv_centred"), sem("conv_scaled"))
        logits1_ready, probs1_mixed, mix1_lo = sem("logits1_ready"), sem("probs1_mixed"), sem("mix1_lo")
        router_logits, router_centred, gates_ready = sem("router_logits"), sem("router_centred"), sem("gates_ready")
        head_root, o_root, pooled = sem("head_root"), sem("o_root"), sem("pooled")
        out_ready = sem("out_ready")
        stored = sem("stored")

        block = ctx.enter_context(nc.Block())

        def bank(o):
            return o % 4

        def down_done(m, kt=FT):
            return (kt * (m + 1) - 1) // BLK

        def q_rows(qt):
            return P if qt < 2 else META

        B2S = B1_CHUNKS % RING
        B2B = B1_OUTS % 4
        assert LAYER_C % RING == 0 and LAYER_O % 4 == 0

        def pair_hi(act, l, pr):
            act.wait_ge(pv_out, l * 24 + 2 * pr + 2)
            act.activation(a_hi[:, pr, :], PS[:, 7, 0:L], ACT.Copy).then_inc(o_hi_done, 1)

        def sig(act, ob, l, k):
            j = (k % 3) * KD + k // 3
            act.wait_ge(out_free, ob + (FFN_UP + KD + QKV_T + j + 1))
            act.activation(G[:, j, :], G[:, j, :], ACT.Sigmoid).then_inc(gate_sig, 1)

        def small_g():
            return small[:, 60:68]

        def B1S(hd, m, qt, k):
            off = (hd % 2) * 6 * P + m * 3 * P + qt * P
            return S_f[:, off:off + k]

        def b1c(hd, c, n=1):
            c += 76 if hd % 2 else 48
            return small[:, c:c + n]

        def pair_lo(dve, l, pr):
            dve.wait_ge(o_hi_done, l * 12 + pr + 1)
            dve.tensor_tensor(a_lo[:, pr, :], PS[:, 7, 0:L], a_hi[:, pr, :].bitcast(F32), ALU.subtract).then_inc(o_lo_done, 1)

        @block.sync
        def _(sp):
            sp.dma_start(raw[:, 0, :], stream[0]).then_inc(raw_landed[0], 16)
            sp.dma_start(col[:, :], cols).then_inc(inputs_landed, 16)
            sp.dma_start(h[:, :, :], xT).then_inc(inputs_landed, 16)
            for s in range(1, RING):
                sp.dma_start(raw[:, s, :], stream[s]).then_inc(raw_landed[s], 16)
            sp.dma_start(mat[:, 0:M_PA], mats[:, 0:M_PA]).then_inc(ones_landed, 16)

            def reload(n, slot):
                sp.wait_ge(lo_done, n - (RING - 1))
                sp.dma_start(raw[:, slot, :], stream[n]).then_inc(raw_landed[slot], 16)

            for n in range(RING, 2 * RING):
                reload(n, n % RING)
            sp.dma_start(mat[:, M_PA:], mats[:, M_PA:]).then_inc(consts_landed, 16)
            sp.dma_start(alibi, b1mats[:, 0:2048].rearrange("p (h t k) -> p h t k", h=4, t=2)).then_inc(consts_landed, 16)
            sp.dma_start(bB[:, 0:1024], b1mats[:, 2048:3072]).then_inc(consts_landed, 16)
            sp.dma_start(PTf[:, 384:640], b1mats[:, 3072:3328]).then_inc(consts_landed, 16)
            with sp.Fori(2, STREAM // RING) as i:
                for s in range(RING):
                    reload(i * RING + s, s)
            for n in range(STREAM // RING * RING, STREAM):
                reload(n, n % RING)
            for m in range(KD):
                sp.wait_ge(out_ready, m + 1)
                sp.dma_start(out[:, m, :], qk[:, m, 0:SEQ]).then_inc(stored, 16)
            sp.wait_ge(stored, 16 * KD)

        ALL_CONSTS = 16 * 4

        @block.scalar
        def _(act):
            def split_hi(n, slot):
                if isinstance(n, int):
                    act.wait_ge(raw_landed[slot], 16 * (n // RING + 1))
                    if n >= RING:
                        act.wait_ge(chunk_used, n - RING + 1)
                else:
                    act.wait_ge(raw_landed[slot], 4 * n + (16 - 4 * slot))
                    act.wait_ge(chunk_used, n - (RING - 1))
                act.activation(w_hi[:, slot, :], raw[:, slot, :], ACT.Copy).then_inc(hi_done, 1)

            def norm_hi(v, m, o):
                act.wait_ge(out_free, o + 1)
                act.activation(x_hi[:, m, :], h[:, m, :], ACT.Copy,
                               scale=col[:, bass.ds(C_G + v * KD + m, 1)]).then_inc(x_hi_done, 1)

            ff = Count()

            def ffn_up(c0, slot0, o, tiles, n_tok, one_split=False):
                def finish(b, f, k):
                    act.wait_ge(a_ready, ff.now + k)
                    act.activation(a_hi[:, bass.ds(f, 1), 0:n_tok], S_sb[:, b, 2:3, 0:n_tok], ACT.Copy)\
                       .then_inc(a_hi_done, 1)

                def turn(c, o, f, first):
                    for s in range(4):
                        if not (first and s == 0 and one_split):
                            split_hi(c + (s + AHEAD), (slot0 + s + AHEAD) % RING)
                        if s == 0 and not first:
                            finish(1, f - 1, 0)
                        if s == 2:
                            finish(0, f, 1)
                        if s % 2 == 1:
                            act.wait_ge(out_free, o + s)
                            act.activation(S_sb[:, s // 2, 0, 0:n_tok], S_sb[:, s // 2, 0, 0:n_tok], ACT.Silu)\
                               .then_inc(act_done, 1)
                    ff.up(2)

                turn(c0, o, 0, True)
                with act.Fori(1, tiles // 2) as i:
                    ff.enter(i, 2, 1)
                    turn(c0 + i * 4, o + i * 4, i * 2, False)
                    ff.leave(tiles // 2 - 1)
                finish(1, tiles - 1, 0)

            def down(c0, slot0, o, kt, v):
                for c in range(kt * KD // BLK):
                    split_hi(c0 + (c + AHEAD), (slot0 + c + AHEAD) % RING)
                    for m in range(KD):
                        if down_done(m, kt) == c and v is not None:
                            norm_hi(v, m, o + m)

            split_hi(0, 0)
            act.wait_ge(inputs_landed, 32)
            for m in range(KD):
                act.activation(x_hi[:, m, :], h[:, m, :], ACT.Copy,
                               scale=col[:, C_G + m:C_G + m + 1]).then_inc(x_hi_done, 1)
            for n in range(1, AHEAD):
                split_hi(n, n)

            for c in range(PEEL1):
                split_hi(c + AHEAD, (c + AHEAD) % RING)
            act.wait_ge(out_free, 4)
            for i in range(2):
                act.activation(qk[:, 2 + i, 0:SEQ], qk[:, 2 + i, 0:SEQ], ACT.Sigmoid).then_inc(conv_gate, 1)
            k = 1
            for c in range(PEEL1, IN1):
                split_hi(c + AHEAD, (c + AHEAD) % RING)
                for _ in range(3 if c > PEEL1 else 0):
                    if k == CONVW:
                        break
                    if k == 1:
                        act.wait_ge(conv_input, 2)
                    if k > 3:
                        act.wait_ge(tap_added, k - 2)
                    act.activation(tap_products[k % 3][:, 0:SEQ], U[:, 1, k:k + SEQ], ACT.Copy,
                                   scale=col[:, C_CONVW + 2 * k + 1:C_CONVW + 2 * k + 2]).then_inc(tap_product, 1)
                    k += 1
                if c < IN1 - 4:
                    continue
                act.wait_ge(out_free, IN1 - 4)
                for t in (2 * (c - IN1 + 4), 2 * (c - IN1 + 4) + 1):
                    act.activation(v_f[:, t * SEQ:(t + 1) * SEQ], qk[:, 6 + t, 0:SEQ], ACT.Square).then_inc(qk_squared, 1)
            act.wait_ge(conv_centred, 1)
            act.activation(YS[:, 0, :], YC[:, 0, :], ACT.Square).then_inc(conv_squared, 1)
            act.wait_ge(aux_free, B1E["conv_mean", 0] + 1)
            act.activation(YS[:, 1, :], YC[:, 1, :], ACT.Square).then_inc(conv_squared, 1)
            act.wait_ge(aux_free, B1E["lambda", 0] + 1)
            act.activation(small[:, 42:44], small[:, 40:42], ACT.Exp).then_inc(lam_exp, 1)

            def head_square(t):
                act.wait_ge(aux_free, B1E["pv", t] + 1)
                act.activation(O2[:, t, :], qk[:, t, 0:SEQ], ACT.Square).then_inc(o_squared, 1)

            for hd in range(HEADS1):
                for m in range(2):
                    for qt in range(2):
                        if qt == 0:
                            act.wait_ge(logits1_ready, 2 * hd + m + 1)
                        else:
                            act.wait_ge(aux_free, B1E[f"score{m}", hd] + 1)
                        k, e = (qt + 1) * P, 2 * m + qt
                        act.activation(B1S(hd, m, qt, k), B1S(hd, m, qt, k), ACT.Exp, scale=-1.0, bias=b1c(hd, e),
                                       accum_out=b1c(hd, 4 + e)).then_inc(exp1_done, 1)
                if hd >= 2:
                    head_square(hd - 2)
            head_square(HEADS1 - 2)
            for i in range(2):
                if i == 0:
                    act.wait_ge(conv_scaled, 1)
                else:
                    act.wait_ge(aux_free, B1E["conv_cast", 0] + 1)
                act.activation(Y[:, i, :], YC[:, i, :], ACT.Silu, scale=col[:, C_LNG + i:C_LNG + i + 1],
                               bias=col[:, C_LNB + i:C_LNB + i + 1]).then_inc(conv_act, 1)
            head_square(HEADS1 - 1)
            for i in range(2):
                k = B1E["pointwise", i]
                act.wait_ge(aux_out, k + 1)
                act.activation(a_hi[:, i, 0:SEQ], PS[:, 4 + k % 4, 0:SEQ], ACT.Identity,
                               bias=col[:, C_PWB + i:C_PWB + i + 1]).then_inc(mix1_hi, 1)
            for i in range(2):
                k = B1E["pool", i]
                act.wait_ge(aux_out, k + 1)
                act.activation(a_hi[:, 2 + i, 0:SEQ], PS[:, 4 + k % 4, 0:SEQ], ACT.Copy,
                               scale=col[:, C_PS + i:C_PS + i + 1]).then_inc(mix1_hi, 1)
            for t in range(HEADS1):
                act.wait_ge(aux_free, B1E["o_cast", t] + 1)
                act.activation(a_hi[:, 4 + t, 0:SEQ], qk[:, t, 0:SEQ], ACT.Copy).then_inc(mix1_hi, 1)
            for c in range(OUT1):
                split_hi(IN1 + c + AHEAD, (IN1 + c + AHEAD) % RING)
                norm_hi(1, c, IN1 + c)
            split_hi(IN1 + OUT1 + AHEAD, (IN1 + OUT1 + AHEAD) % RING)
            act.wait_ge(router_centred, 1)
            act.activation(small_g(), small_g(), ACT.Exp).then_inc(router_exp, 1)
            act.wait_ge(router_centred, 2)
            act.activation(small[:, 90:92], small[:, 90:92], ACT.Exp).then_inc(router_exp, 1)
            cb, ob = IN1 + OUT1, IN1 + OUT1
            for half in range(2):
                ffn_up(cb, cb % RING, ob, MOE_HALF, SEQ, half == 0)
                down(cb + 2 * MOE_HALF, (cb + 2 * MOE_HALF) % RING, ob + 2 * MOE_HALF, MOE_HALF, 2 if half else None)
                cb += MOE_C
                ob += 2 * MOE_HALF + KD

            with act.Fori(0, LAYERS) as l:
                cb = l * LAYER_C + B1_CHUNKS
                ob = l * LAYER_O + B1_OUTS
                sl, bk = B2S, 0
                ff.enter(l, 2 * FT)
                ffn_up(cb, sl, ob, FT, L)
                down(cb + FFN_UP, (sl + FFN_UP) % RING, ob + FFN_UP, FT, l * 3 + 3)
                c, o = FFN_C, FFN_UP + KD
                for t, (kind, i) in enumerate(QKV_ORDER):
                    split_hi(cb + (c + t + AHEAD), (sl + c + t + AHEAD) % RING)
                    if kind in ("kC", "qC"):
                        e = 0 if kind == "kC" else 1 + i
                        act.wait_ge(out_free, ob + (o + t + 1))
                        act.activation(G[:, e, :], qk[:, R_OF[kind] + i, :], ACT.Square).then_inc(c_squared, 1)
                c, o = c + QKV_T, o + QKV_T
                nexp = Count()

                def turned(j):
                    act.wait_ge(probsT_out, l * 24 + j + 1)
                    act.activation(PT[:, 1, :], PS[:, 6, 0:L], ACT.Copy).then_inc(probsT_act, 1)
                    act.activation(PT[0:META, 2, P:2 * P], PS[0:META, 6, L:L + P], ACT.Copy).then_inc(probsT_act, 1)

                for j in range(24):
                    split_hi(cb + (c + j + AHEAD), (sl + c + j + AHEAD) % RING)
                    if 7 <= j < 15:
                        if j >= 9:
                            act.wait_ge(logits_ready, l * 72 + 3 * (j - 1) + 3)
                        hB = j - 7
                        for r in range(4):
                            src = bass.AP(rpbz.tensor, l * (8 * 7 * SKEW) + ((hB * 7 + 3 - r) * SKEW + 63),
                                          [[127, 64], [SKEW, 4], [1, 64]])
                            p0 = 64 * (r % 2)
                            act.dma_start(biasB[p0:p0 + 64, hB % 2, r // 2, 0:SEQ].rearrange("p (a b) -> p a b", a=4),
                                          src).then_inc(bias_landed[hB % 2], 16)
                    if j % 2 == 1 and j > 1:
                        pair_hi(act, l, (j - 3) // 2)
                    if j > 0:
                        turned(j - 1)
                    for qt in range(3):
                        r = q_rows(qt)
                        act.wait_ge(logits_ready, l * 72 + 3 * j + qt + 1)
                        act.activation(S_sb[0:r, j % 2, qt, :], S_sb[0:r, j % 2, qt, :], ACT.Exp, scale=-1.0,
                                       bias=minl[0:r, 3 * (j % 2) + qt:3 * (j % 2) + qt + 1],
                                       accum_out=rsum[0:r, 3 * (j % 2) + qt:3 * (j % 2) + qt + 1]).then_inc(exp_done, nexp.up())
                    if j < 8:
                        hA = j // 2 + 4 * (j % 2)
                        act.activation(esink[:, 3 * (j % 2):3 * (j % 2) + 3], minl[:, 3 * (j % 2):3 * (j % 2) + 3], ACT.Exp,
                                       bias=col[:, bass.ds(l * 8 + C_SINK + hA, 1)]).then_inc(exp_done, nexp.up())
                turned(23)
                pair_hi(act, l, 11)
                assert nexp.n == 80
                for k in range(3):
                    sig(act, ob, l, k)
                c, o = c + GATE_T, o + GATE_T
                done = 3

                def mixed_hi(m):
                    act.wait_ge(mixed_ready, l * KD + m + 1)
                    act.activation(a_hi[:, 12 + m, :], S_sb[:, m % 2, 0, :], ACT.Copy).then_inc(mix_hi_done, 1)

                for s in range(BRANCH_C):
                    split_hi(cb + (c + s + AHEAD), (sl + c + s + AHEAD) % RING)
                    while done < min(24, 2 * s + 5):
                        sig(act, ob, l, done)
                        done += 1
                    for u in (2 * s - 2, 2 * s - 1):
                        if u > 0 and u % 3 == 2:
                            mixed_hi(u // 3)
                mixed_hi(KD - 1)
                c, o = c + BRANCH_C, o + 3 * KD
                for m in range(OUT_C):
                    split_hi(cb + (c + m + AHEAD), (sl + c + m + AHEAD) % RING)
                    norm_hi(l * 3 + 4, m, ob + (o + m))
                c, o = c + OUT_C, o + KD
                ffn_up(cb + c, (sl + c) % RING, ob + o, FT, L)
                down(cb + (c + FFN_UP), (sl + c + FFN_UP) % RING, ob + (o + FFN_UP), FT, l * 3 + 5)
                ff.leave(LAYERS)

        @block.tensor
        def _(pe):
            ax = Count()

            def aux_begin():
                k = ax.n
                if not (isinstance(ax.now, int) and k < 4):
                    pe.wait_ge(aux_free, ax.now - 3)
                return 4 + k % 4

            def aux_end(mm):
                mm.then_inc(aux_out, ax.up())

            def product(ps, slot, b, rh, rl, first, last):
                hi, lo = w_hi[:, slot, b * P:(b + 1) * P], w_lo[:, slot, b * P:(b + 1) * P]
                pe.matmul(ps, hi, rh, start=first, stop=False)
                pe.matmul(ps, hi, rl, start=False, stop=False)
                return pe.matmul(ps, lo, rh, start=False, stop=last)

            def chunk8(n, slot, o, bk, n_tok, xh, xl, ready=None, lag=4):
                pe.wait_ge(lo_done, n + 1)
                if not isinstance(o, int) or o >= lag:
                    pe.wait_ge(out_free, o - (lag - 1))
                ps = PS[:, bk, 0:n_tok]
                for kt in range(KD):
                    if ready is not None:
                        pe.wait_ge(ready[0], ready[1] + (kt + 1))
                    mm = product(ps, slot, kt, xh[:, kt, 0:n_tok], xl[:, kt, 0:n_tok], kt == 0, kt == KD - 1)
                mm.then_inc(chunk_used, 1)

            def stat(v):
                b = aux_begin()
                pe.wait_ge(squares_summed, v + 1)
                aux_end(pe.matmul(PS[:, b, 0:L], ones, acc, start=True, stop=True))

            def ffn_up(cb, slot0, ob, bk0, tiles, n_tok, v=None, beside=None):
                def turn(c, o, first):
                    for s in range(4):
                        chunk8(c + s, (slot0 + s) % RING, o + s, (bk0 + s) % 4, n_tok, x_hi, x_lo,
                               (x_lo_done, v * KD) if first and s == 0 and v is not None else None)
                        if first and s == 0 and v is not None:
                            stat(v)
                        if first and beside is not None:
                            beside(s)
                turn(cb, ob, True)
                with pe.Fori(1, tiles // 2) as i:
                    turn(cb + i * 4, ob + i * 4, False)

            def down(cb, slot0, ob, bk0, kt, n_tok, abase, beside=None):
                blk = 0
                for m in range(KD):
                    for k in range(kt):
                        c, b = blk // BLK, blk % BLK
                        if b == 0:
                            pe.wait_ge(lo_done, cb + (c + 1))
                        if k == 0:
                            pe.wait_ge(out_free, ob + (m - 3))
                        if m == 0:
                            pe.wait_ge(a_lo_done, abase + (k + 1))
                        mm = product(PS[:, (bk0 + m) % 4, 0:n_tok], (slot0 + c) % RING, b,
                                     a_hi[:, k, 0:n_tok], a_lo[:, k, 0:n_tok], k == 0, k == kt - 1)
                        if b == BLK - 1:
                            mm.then_inc(chunk_used, 1)
                        blk += 1
                    if beside is not None:
                        beside(m)

            for c in range(PEEL1):
                chunk8(c, c % RING, c, bank(c), SEQ, x_hi, x_lo, (x_lo_done, 0) if c == 0 else None)
                if c == 2:
                    pe.wait_ge(ones_landed, 16)
                    b = aux_begin()
                    pe.wait_ge(squares_summed, 1)
                    pe.matmul(PS[:, b, 0:L], ones, acc, start=True, stop=False)
                    pe.wait_ge(half_summed, 1)
                    aux_end(pe.matmul(PS[:, b, 0:L], ones, half_acc, start=False, stop=True))
            with pe.Fori(0, (IN1 - PEEL1) // 4) as i:
                for s in range(4):
                    c = i * 4 + (PEEL1 + s)
                    chunk8(c, (PEEL1 + s) % RING, c, bank(PEEL1 + s), SEQ, x_hi, x_lo)
            pe.wait_ge(consts_landed, ALL_CONSTS)
            b = aux_begin()
            for i in range(2):
                pe.wait_ge((conv_done, conv1_done)[i], 1)
                mm = pe.matmul(PS[:, b, 0:SEQ], ones, Y[:, i, :], start=(i == 0), stop=(i == 1))
            aux_end(mm)
            b = aux_begin()
            pe.wait_ge(qk_squared, 8)
            for t in range(8):
                pe.matmul(PS[0:17, b, 0:SEQ], mat[:, M_SEL16 + 17 * t:M_SEL16 + 17 * t + 17],
                          v_f[:, t * SEQ:(t + 1) * SEQ], start=(t == 0), stop=False)
            for i in range(2):
                pe.wait_ge(conv_squared, i + 1)
                mm = pe.matmul(PS[0:17, b, 0:SEQ], mat[:, M_SEL16 + 17 * 8:M_SEL16 + 17 * 9], YS[:, i, :],
                               start=False, stop=(i == 1))
            aux_end(mm)
            b = aux_begin()
            pe.wait_ge(lam_products, 1)
            aux_end(pe.matmul(PS[:, b, 0:2], ones[0:64, :], small[0:64, 38:40], start=True, stop=True))

            pe.wait_ge(head_root, 1)
            pe.wait_ge(spread_landed, 16)
            for t in range(8):
                b = aux_begin()
                aux_end(pe.matmul(PS[:, b, 0:SEQ], spread_sb[:, t * P:(t + 1) * P], head_rs[0:16, :], start=True, stop=True))

            def scores(hd):
                for m in range(2):
                    b = aux_begin()
                    o = 64 * m
                    pe.matmul(PS[:, b, 0:P], qk[o:o + 64, 6 + hd, 0:P], qk[o:o + 64, 10 + hd, 0:P], start=True, stop=True)
                    aux_end(pe.matmul(PS[:, b, P:3 * P], qk[o:o + 64, 6 + hd, P:2 * P], qk[o:o + 64, 10 + hd, 0:SEQ],
                                      start=True, stop=True))

            pe.wait_ge(aux_free, B1E["qk_cast", 7] + 1)
            scores(0)
            for t in range(HEADS1):
                b = aux_begin()
                for kt in range(2):
                    mm = pe.transpose(PS[:, b, kt * P:(kt + 1) * P], qk[:, 14 + t, kt * P:(kt + 1) * P], ident)
                aux_end(mm)
            b = aux_begin()
            aux_end(pe.matmul(PS[:, b, 0:SEQ], ident[0:17, 16:17].to_broadcast([17, P]), head_rs, start=True, stop=True))
            scores(1)
            for hd in range(HEADS1):
                b = aux_begin()
                pe.wait_ge(probs1_mixed, 2 * hd + 2)
                pe.transpose(PS[:, b, 0:P], B1S(hd, 0, 0, P), ident)
                pe.transpose(PS[:, b, P:2 * P], B1S(hd, 0, 1, P), ident)
                aux_end(pe.transpose(PS[:, b, 2 * P:3 * P], B1S(hd, 0, 1, SEQ)[:, P:2 * P], ident))
                if hd + 2 < HEADS1:
                    scores(hd + 2)
                b = aux_begin()
                pe.wait_ge(aux_free, B1E["turn", hd] + 1)
                pe.matmul(PS[:, b, 0:SEQ], v_tok[:, 0, hd * P:(hd + 1) * P], PTf[:, 0:SEQ], start=True, stop=True,
                          skip_group_check=True)
                aux_end(pe.matmul(PS[:, b, P:SEQ], v_tok[:, 1, hd * P:(hd + 1) * P], PTf[:, SEQ:SEQ + P],
                                  start=False, stop=True, skip_group_check=True))
            b = aux_begin()
            pe.wait_ge(o_squared, 4)
            for t in range(HEADS1):
                mm = pe.matmul(PS[0:4, b, 0:SEQ], mat[:, M_SEL4 + 4 * t:M_SEL4 + 4 * t + 4], O2[:, t, :],
                               start=(t == 0), stop=(t == 3))
            aux_end(mm)
            pe.wait_ge(conv_act, 2)
            for m in range(2):
                b = aux_begin()
                for k in range(2):
                    mm = pe.matmul(PS[:, b, 0:SEQ], pw_w[:, k, m * P:(m + 1) * P], Y[:, k, :], start=(k == 0), stop=(k == 1))
                aux_end(mm)
            pe.wait_ge(pooled, 1)
            for m in range(2):
                b = aux_begin()
                aux_end(pe.matmul(PS[:, b, 0:SEQ], pool_w[:, m, :], qk[:, 4 + m, 0:SEQ], start=True, stop=True))
            pe.wait_ge(o_root, 1)
            for t in range(HEADS1):
                b = aux_begin()
                aux_end(pe.matmul(PS[:, b, 0:SEQ], ident[0:4, t:t + 1].to_broadcast([4, P]), S_f[0:4, 256:512],
                                  start=True, stop=True))
            for c in range(OUT1):
                n = IN1 + c
                if c == 0:
                    pe.wait_ge(aux_free, B1E["pool", 1] + 1)
                    pe.wait_ge(mix1_lo, HEADS1)
                chunk8(n, n % RING, n, bank(n), SEQ, a_hi, a_lo)
            stat(1)
            b = aux_begin()
            for k in range(KD):
                pe.wait_ge(out_free, IN1 + k + 1)
                pe.wait_ge(x_lo_done, KD + k + 1)
                mm = pe.matmul(PS[0:20, b, 0:SEQ], col[:, C_RW + 20 * k:C_RW + 20 * k + 20], qk[:, 8 + k, 0:SEQ],
                               start=(k == 0), stop=(k == KD - 1))
            aux_end(mm)

            def beside_first_turn(s):
                if s == 0:
                    b = aux_begin()
                    pe.wait_ge(router_logits, 1)
                    for t in range(2):
                        mm = pe.transpose(PS[:, b, 20 * t:20 * t + 20], S_f[0:20, t * P:(t + 1) * P], ident[0:20, 0:20])
                    aux_end(mm)
                if s == 3:
                    b = aux_begin()
                    pe.wait_ge(gates_ready, 2)
                    for t in range(2):
                        mm = pe.transpose(PS[0:16, b, t * P:(t + 1) * P], S_f[:, 600 + 16 * t:616 + 16 * t], ident)
                    aux_end(mm)
                    pe.wait_ge(aux_free, B1E["gates_turn", 0] + 1)
                    gates_cast(0)

            def gates_cast(half):
                for e in range(4 * half, 4 * half + 4):
                    b = aux_begin()
                    for u in range(2):
                        mm = pe.matmul(PS[:, b, u * SEQ:(u + 1) * SEQ],
                                       ident[0:16, 2 * e + u:2 * e + u + 1].to_broadcast([16, P]),
                                       gates_T, start=True, stop=True)
                    aux_end(mm)

            cb, ob, ab = IN1 + OUT1, IN1 + OUT1, 0
            for half in range(2):
                ffn_up(cb, cb % RING, ob, bank(ob), MOE_HALF, SEQ, beside=None if half else beside_first_turn)
                down(cb + 2 * MOE_HALF, (cb + 2 * MOE_HALF) % RING, ob + 2 * MOE_HALF, bank(ob + 2 * MOE_HALF),
                     MOE_HALF, SEQ, ab, beside=None if half else (lambda m: gates_cast(1) if m == 1 else None))
                cb += MOE_C
                ob += 2 * MOE_HALF + KD
                ab += MOE_HALF
            assert ax.n == B1_AUX, (ax.n, B1_AUX)

            castC_at = B1_AUX + CASTC_IN_LAYER
            with pe.Fori(0, LAYERS) as l:
                ax.enter(l, LAYER_A)
                cb = l * LAYER_C + B1_CHUNKS
                ob = l * LAYER_O + B1_OUTS
                sl, bk = B2S, B2B
                ab = l * (2 * FT) + MOE_T
                ffn_up(cb, sl, ob, bk, FT, L, l * 3 + 2)
                down(cb + FFN_UP, (sl + FFN_UP) % RING, ob + FFN_UP, (bk + FFN_UP) % 4, FT, L, ab)
                c, o = FFN_C, FFN_UP + KD
                for t, (kind, i) in enumerate(QKV_ORDER):
                    chunk8(cb + (c + t), (sl + c + t) % RING, ob + (o + t), (bk + o + t) % 4, L, x_hi, x_lo,
                           (x_lo_done, (l * 3 + 3) * KD) if t == 0 else None)
                    for what, i in QKV_EVENTS.get(t, []):
                        if what == "stat":
                            stat(l * 3 + 3)
                            continue
                        b = aux_begin()
                        if what in ("swapA", "swapC"):
                            if what == "swapA":
                                tt = 0 if i == R_KA else 16 + i - R_QA
                                pe.wait_ge(out_free, ob + (o + tt + 1))
                            else:
                                pe.wait_ge(aux_free, ax.term + (castC_at + C_TILES.index(i) + 1))
                            perm = mat[:, M_PA:M_PA + P] if what == "swapA" else mat[:, M_PC:M_PC + P]
                            mm = pe.matmul(PS[:, b, 0:L], perm, qk[:, i, :], start=True, stop=True)
                        elif what == "v":
                            pe.wait_ge(out_free, ob + (o + 6 + i + 1))
                            vs = vstage[i % 2]
                            pe.transpose(PS[:, b, 0:P], vs[:, 0:P], ident)
                            pe.transpose(PS[:, b, P:2 * P], vs[:, P:2 * P], ident)
                            mm = pe.transpose(PS[0:META, b, 2 * P:3 * P], vs[:, 2 * P:L], ident)
                        elif what == "sumC":
                            pe.wait_ge(c_squared, l * 5 + 5)
                            for e in range(5):
                                mm = pe.matmul(PS[0:10, b, 0:L], mat[:, M_SEL16 + 17 * e:M_SEL16 + 17 * e + 10],
                                               G[:, e, :], start=(e == 0), stop=(e == 4))
                        else:
                            pe.wait_ge(c_rstd, l + 1)
                            for u in range(2):
                                mm = pe.matmul(PS[64 * u:64 * u + 64, b, 0:L],
                                               ident[0:10, 2 * i + u:2 * i + u + 1].to_broadcast([10, 64]),
                                               G[0:10, 9, :], start=True, stop=True)
                        aux_end(mm)
                c, o = c + QKV_T, o + QKV_T
                pe.wait_ge(out_free, ob + o)
                pe.wait_ge(aux_free, ax.now)
                pe.wait_ge(roped, l * 10 + 5)

                def pv(j):
                    t, b = j // 2 % 4, j % 2
                    typ = j // 8
                    vcol = (2 + t if typ == 1 else (0 if typ == 0 else 1)) * P + 64 * b
                    pe.wait_ge(probsT_dve, l * 72 + 3 * j + 3)
                    pe.wait_ge(probsT_act, l * 48 + 2 * j + 2)
                    if b == 0 and j > 0:
                        pe.wait_ge(o_lo_done, l * 12 + j // 2)
                    for kt in range(3):
                        r = q_rows(kt)
                        mm = pe.matmul(PS[64 * b:64 * b + 64, 7, 0:L], v_tok[0:r, kt, vcol:vcol + 64], PT[0:r, kt, :],
                                       start=(kt == 0), stop=(kt == 2))
                    mm.then_inc(pv_out, 1)

                def turn(j):
                    for n, (kt, qt) in enumerate([(0, 0), (0, 1), (1, 0), (0, 2), (1, 1), (1, 2)]):
                        r = q_rows(qt)
                        if n < 3:
                            pe.wait_ge(probs_ready, l * 72 + 3 * j + n + 1)
                        pe.transpose(PS[:, 5 + kt, qt * P:qt * P + r], S_sb[0:r, j % 2, qt, kt * P:(kt + 1) * P],
                                     ident[0:r, 0:r])
                    pe.transpose(PS[0:META, 5, L:L + P], S_sb[:, j % 2, 0, 2 * P:L], ident)
                    pe.transpose(PS[0:META, 6, L:L + P], S_sb[:, j % 2, 1, 2 * P:L], ident)
                    pe.transpose(PS[0:META, 5, L + P:L + P + META], S_sb[0:META, j % 2, 2, 2 * P:L],
                                 ident[0:META, 0:META]).then_inc(probsT_out, 1)

                for j in range(24):
                    t, b = j // 2 % 4, j % 2
                    typ = j // 8
                    rq = (R_QA, R_QB, R_QC)[typ] + t
                    rk = (R_KA, R_KB + t, R_KC)[typ]
                    lo, hi = 64 * b, 64 * b + 64
                    if typ == 2 and t == 0 and b == 0:
                        pe.wait_ge(roped, l * 10 + 10)
                    if j > 0:
                        pe.wait_ge(logits_ready, l * 72 + 3 * j)
                    for qt in range(3):
                        r = q_rows(qt)
                        pe.matmul(PS[0:r, 2 + qt, 0:L], qk[lo:hi, rq, qt * P:qt * P + r], qk[lo:hi, rk, :],
                                  start=True, stop=True).then_inc(scores_out, 1)
                    if j > 0:
                        turn(j - 1)
                    chunk8(cb + (c + j), (sl + c + j) % RING, ob + (o + j), j % 2, L, x_hi, x_lo, lag=2)
                    if j > 0:
                        pv(j - 1)
                turn(23)
                pv(23)
                c, o = c + GATE_T, o + GATE_T
                pe.wait_ge(out_free, ob + o)
                for u in range(3 * KD):
                    s = u // 2
                    if u % 2 == 0:
                        pe.wait_ge(lo_done, cb + (c + s + 1))
                    pe.wait_ge(out_free, ob + (o + u - 3))
                    n = u % 3
                    if u < 3:
                        pe.wait_ge(o_lo_done, l * 12 + 4 * n + 4)
                    for k in range(4):
                        mm = product(PS[:, (bk + o + u) % 4, 0:L], (sl + c + s) % RING, 4 * (u % 2) + k,
                                     a_hi[:, 4 * n + k, :], a_lo[:, 4 * n + k, :], k == 0, k == 3)
                    if u % 2 == 1:
                        mm.then_inc(chunk_used, 1)
                c, o = c + BRANCH_C, o + 3 * KD
                for m in range(OUT_C):
                    chunk8(cb + (c + m), (sl + c + m) % RING, ob + (o + m), (bk + o + m) % 4, L,
                           a_hi[:, 12:20, :], a_lo[:, 12:20, :], (mix_lo_done, l * KD) if m == 0 else None)
                c, o = c + OUT_C, o + KD
                ffn_up(cb + c, (sl + c) % RING, ob + o, (bk + o) % 4, FT, L, l * 3 + 4)
                down(cb + (c + FFN_UP), (sl + c + FFN_UP) % RING, ob + (o + FFN_UP), (bk + o + FFN_UP) % 4, FT, L, ab + FT)
                ax.leave(LAYERS)
            stat(8)

        @block.vector
        def _(dve):
            st = Count()
            ax = Count()

            def step(ins):
                ins.then_inc(dve_step, st.up())
                dve.wait_ge(dve_step, st.now)

            def split_lo(n, slot):
                dve.wait_ge(hi_done, n + 1)
                dve.tensor_tensor(w_lo[:, slot, :], raw[:, slot, :], w_hi[:, slot, :].bitcast(F32),
                                  ALU.subtract).then_inc(lo_done, 1)

            def norm_lo(v, m):
                dve.wait_ge(x_hi_done, v * KD + (m + 1))
                dve.scalar_tensor_tensor(x_lo[:, m, :], h[:, m, :], col[:, bass.ds(C_G + v * KD + m, 1)],
                                         x_hi[:, m, :].bitcast(F32), ALU.mult, ALU.subtract).then_inc(x_lo_done, 1)

            def aux_bank():
                dve.wait_ge(aux_out, ax.now + 1)
                return 4 + ax.n % 4

            def inverse_root(x, y, done, k):
                n, r = x.shape[1], x.shape[0]
                t0, t1 = G[0:r, 21, 0:n], G[0:r, 23, 0:n]
                dve.wait_ge(aux_free, ax.now)
                step(dve.tensor_scalar(t0.bitcast(I32), x.bitcast(I32), 1, None, ALU.logical_shift_right))
                step(dve.tensor_scalar(y.bitcast(I32), t0.bitcast(I32), -1.0, float(0x5F3759DF), ALU.mult, ALU.add))
                for i in range(3):
                    step(dve.tensor_tensor(t0, y, y, ALU.mult))
                    step(dve.scalar_tensor_tensor(t1, t0, -0.5, x, ALU.mult, ALU.mult))
                    ins = dve.scalar_tensor_tensor(y, t1, 1.5, y, ALU.add, ALU.mult)
                    if i < 2:
                        step(ins)
                    else:
                        ins.then_inc(done, k)

            def mean_square(v):
                b = aux_bank()
                dve.tensor_scalar(ms, PS[:, b, 0:L], 1.0 / D, EPS, ALU.mult, ALU.add).then_inc(aux_free, ax.up())
                inverse_root(ms, rstd[:, :], rstd_done, 1)
                dve.wait_ge(rstd_done, v + 1)

            def residual(v, m, o, bk, coef, n_tok):
                dve.scalar_tensor_tensor(h[:, m, 0:n_tok], PS[:, bk, 0:n_tok], coef, h[:, m, 0:n_tok],
                                         ALU.mult, ALU.add).then_inc(out_free, 1)
                if v is not None:
                    dve.wait_ge(out_free, o + 1)
                    norm_lo(v, m)

            ff = Count()

            def ffn_up(cb, slot0, ob, bk0, tiles, n_tok, v=None, experts=None, one_split=False):
                def finish(b, f, k):
                    dve.wait_ge(a_hi_done, ff.now + k)
                    dve.tensor_tensor(a_lo[:, bass.ds(f, 1), 0:n_tok], S_sb[:, b, 2:3, 0:n_tok],
                                      a_hi[:, bass.ds(f, 1), 0:n_tok].bitcast(F32), ALU.subtract).then_inc(a_lo_done, 1)

                def turn(c, o, i, first):
                    f = i * 2
                    for s in range(4):
                        if not (first and s == 0 and one_split):
                            split_lo(c + (s + AHEAD), (slot0 + s + AHEAD) % RING)
                        if s == 0 and not first:
                            finish(1, f - 1, 0)
                        if s == 2:
                            finish(0, f, 1)
                        if first and s == 0 and v is not None:
                            mean_square(v)
                        b = s // 2
                        dve.wait_ge(chunk_used, c + (s + 1))
                        ps = PS[:, (bk0 + s) % 4, 0:n_tok]
                        if s % 2 == 0:
                            dve.tensor_tensor(S_sb[:, b, 0, 0:n_tok], ps, rstd[:, 0:n_tok], ALU.mult).then_inc(out_free, 1)
                            continue
                        scale = rstd[:, 0:n_tok] if experts is None else gates_bc[:, bass.ds(i + experts, 1), :]
                        up = S_sb[:, b, 1:2, 0:n_tok]
                        if experts is None:
                            dve.tensor_tensor(S_sb[:, b, 1, 0:n_tok], ps, scale, ALU.mult).then_inc(out_free, 1)
                        else:
                            dve.tensor_tensor(up, PS[:, (bk0 + s) % 4:(bk0 + s) % 4 + 1, 0:n_tok], scale, ALU.mult)\
                               .then_inc(out_free, 1)
                        dve.wait_ge(out_free, o + (s + 1))
                        dve.wait_ge(act_done, ff.now + (b + 1))
                        dve.tensor_tensor(S_sb[:, b, 2, 0:n_tok], S_sb[:, b, 0, 0:n_tok], S_sb[:, b, 1, 0:n_tok],
                                          ALU.mult).then_inc(a_ready, 1)
                    ff.up(2)
                turn(cb, ob, 0, True)
                with dve.Fori(1, tiles // 2) as i:
                    ff.enter(i, 2, 1)
                    turn(cb + i * 4, ob + i * 4, i, False)
                    ff.leave(tiles // 2 - 1)
                finish(1, tiles - 1, 0)

            def down(cb, slot0, ob, bk0, kt, coef, v, n_tok, beside=None):
                for c in range(kt * KD // BLK):
                    split_lo(cb + (c + AHEAD), (slot0 + c + AHEAD) % RING)
                    for m in range(KD):
                        if down_done(m, kt) == c:
                            dve.wait_ge(chunk_used, cb + (c + 1))
                            residual(v, m, ob + m, (bk0 + m) % 4, coef, n_tok)
                            if beside is not None:
                                beside(m)

            dve.memset(small[:, :], 0.0).then_inc(dve_step, st.up())
            dve.wait_ge(dve_step, st.now)
            step(dve.memset(small[:, 12:36], 1.0))
            step(dve.memset(U[:, :, 0:CONVW - 1], 0.0))
            step(dve.memset(UP[:, :, 0:16], 0.0))
            dve.memset(zero, 0.0).then_inc(setup_done, 1)
            split_lo(0, 0)
            dve.wait_ge(inputs_landed, 32)
            for m in range(KD):
                norm_lo(0, m)
            for n in range(1, AHEAD):
                split_lo(n, n)
            for m in range(KD // 2, KD):
                half_sq = half_acc if m == KD // 2 else G[:, 18, :]
                step(dve.tensor_tensor(half_sq, h[:, m, :], h[:, m, :], ALU.mult))
                if m > KD // 2:
                    ins = dve.tensor_tensor(half_acc, half_acc, half_sq, ALU.add)
                    if m < KD - 1:
                        step(ins)
                    else:
                        ins.then_inc(half_summed, 1)

            def in_tile(t, bk, chunk):
                dve.wait_ge(chunk_used, chunk + 1)
                dve.tensor_tensor(qk[:, bass.ds(t, 1), 0:SEQ], PS[:, bk:bk + 1, 0:SEQ],
                                  rstd[:, 0:SEQ].unsqueeze(1), ALU.mult).then_inc(out_free, 1)

            for c in range(PEEL1):
                if c != 1:
                    split_lo(c + AHEAD, (c + AHEAD) % RING)
                if c == 0:
                    split_lo(1 + AHEAD, (1 + AHEAD) % RING)
                    mean_square(0)
                in_tile(c, bank(c), c)
            tap = 0
            for c in range(PEEL1, IN1):
                split_lo(c + AHEAD, (c + AHEAD) % RING)
                in_tile(c, bank(c), c)
                for _ in range(3 if c > PEEL1 else 0):
                    if tap == CONVW:
                        break
                    u, w = U[:, 0, tap:tap + SEQ], col[:, C_CONVW + 2 * tap:C_CONVW + 2 * tap + 1]
                    total = YC[:, 0, :] if tap % 2 else Y[:, 0, :]
                    if tap == 0:
                        dve.wait_ge(conv_input, 1)
                        ins = dve.tensor_scalar(total, u, w, col[:, C_CONVB:C_CONVB + 1], ALU.mult, ALU.add)
                    elif tap == 1:
                        ins = dve.tensor_scalar(total, u, w, None, ALU.mult)
                    else:
                        dve.wait_ge(dve_step, st.now - 1)
                        ins = dve.scalar_tensor_tensor(total, u, w, total, ALU.mult, ALU.add)
                    ins.then_inc(dve_step, st.up())
                    tap += 1
            assert tap == CONVW
            dve.wait_ge(dve_step, st.now)
            dve.tensor_tensor(Y[:, 0, :], Y[:, 0, :], YC[:, 0, :], ALU.add).then_inc(conv_done, 1)
            dve.wait_ge(consts_landed, ALL_CONSTS)
            lam_in = col[0:64, C_LAM:C_LAM + 4].rearrange("p (a b) -> p a b", a=2)
            dve.tensor_tensor(small[0:64, 38:40].unsqueeze(2), lam_in[:, :, 0:1], lam_in[:, :, 1:2], ALU.mult)\
               .then_inc(lam_products, 1)
            b = aux_bank()
            for i in range(2):
                ins = dve.scalar_tensor_tensor(YC[:, i, :], PS[:, b, 0:SEQ], -1.0 / 256, Y[:, i, :], ALU.mult, ALU.add)
                if i == 0:
                    ins.then_inc(conv_centred, 1)
                else:
                    ins.then_inc(aux_free, ax.up())
            b = aux_bank()
            dve.tensor_scalar(head_ms, PS[0:17, b, 0:SEQ], 1.0 / HD, EPS, ALU.mult, ALU.add).then_inc(aux_free, ax.up())
            inverse_root(head_ms, head_rs, head_root, 1)
            b = aux_bank()
            dve.tensor_copy(small[:, 40:42], PS[:, b, 0:2]).then_inc(aux_free, ax.up())
            for t in range(8):
                b = aux_bank()
                g = C_QN1 + t // 4
                dve.scalar_tensor_tensor(qk[:, 6 + t, 0:SEQ], qk[:, 6 + t, 0:SEQ], col[:, g:g + 1], PS[:, b, 0:SEQ],
                                         ALU.mult, ALU.mult).then_inc(aux_free, ax.up())

            def logits(hd):
                for m in range(2):
                    b = aux_bank()
                    for qt in range(2):
                        k, e = (qt + 1) * P, 2 * m + qt
                        ins = dve.tensor_tensor_reduce(B1S(hd, m, qt, k), PS[:, b, qt * P:qt * P + k], alibi[:, hd, qt, 0:k],
                                                       -0.125, 3.0e38, ALU.add, ALU.min, b1c(hd, e))
                        if qt == 0:
                            ins.then_inc(logits1_ready, 1)
                        else:
                            ins.then_inc(aux_free, ax.up())

            logits(0)
            for t in range(HEADS1):
                b = aux_bank()
                dve.tensor_copy(v_tok[:, 0:2, t * P:(t + 1) * P],
                                PS[:, b, 0:2 * P].rearrange("p (k c) -> p k c", k=2)).then_inc(aux_free, ax.up())
            b = aux_bank()
            for i in range(2):
                ins = dve.tensor_tensor(YC[:, i, :], YC[:, i, :], PS[:, b, 0:SEQ], ALU.mult)
                if i == 0:
                    ins.then_inc(conv_scaled, 1)
                else:
                    ins.then_inc(aux_free, ax.up())
            dve.wait_ge(lam_exp, 1)
            step(dve.tensor_tensor(small[:, 47:48], small[:, 42:43], small[:, 43:44], ALU.subtract))
            step(dve.tensor_scalar(small[:, 47:48], small[:, 47:48], LAM_INIT, None, ALU.add))
            dve.wait_ge(pooled, 1)
            logits(1)

            def mix_maps(hd):
                dve.wait_ge(exp1_done, 4 * (hd + 1))
                step(dve.reciprocal(b1c(hd, 8, 4), b1c(hd, 4, 4)))
                step(dve.tensor_scalar(b1c(hd, 10, 2), b1c(hd, 10, 2), small[:, 47:48], None, ALU.mult))
                for qt in range(2):
                    k = (qt + 1) * P
                    step(dve.tensor_scalar(B1S(hd, 1, qt, k), B1S(hd, 1, qt, k), b1c(hd, 10 + qt), None, ALU.mult))
                    dve.scalar_tensor_tensor(B1S(hd, 0, qt, k), B1S(hd, 0, qt, k), b1c(hd, 8 + qt), B1S(hd, 1, qt, k),
                                             ALU.mult, ALU.subtract).then_inc(probs1_mixed, 1)

            mix_maps(0)
            for hd in range(HEADS1):
                b = aux_bank()
                dve.tensor_copy(PTf[:, 0:3 * P], PS[:, b, 0:3 * P]).then_inc(aux_free, ax.up())
                if hd + 2 < HEADS1:
                    logits(hd + 2)
                if hd + 1 < HEADS1:
                    mix_maps(hd + 1)
                b = aux_bank()
                dve.tensor_copy(qk[:, hd, 0:SEQ], PS[:, b, 0:SEQ]).then_inc(aux_free, ax.up())
            keep = (1.0 - LAM_INIT) ** 2
            b = aux_bank()
            dve.tensor_scalar(S_f[0:4, 0:SEQ], PS[0:4, b, 0:SEQ], 1.0 / (P * keep), EPS / keep, ALU.mult, ALU.add)\
               .then_inc(aux_free, ax.up())
            inverse_root(S_f[0:4, 0:SEQ], S_f[0:4, 256:512], o_root, 1)
            for i in range(2):
                dve.wait_ge(mix1_hi, i + 1)
                b = aux_bank()
                dve.scalar_tensor_tensor(a_lo[:, i, 0:SEQ], PS[:, b, 0:SEQ], col[:, C_PWB + i:C_PWB + i + 1],
                                         a_hi[:, i, 0:SEQ].bitcast(F32), ALU.add, ALU.subtract).then_inc(aux_free, ax.up())
            for i in range(2):
                dve.wait_ge(mix1_hi, 2 + i + 1)
                b = aux_bank()
                dve.scalar_tensor_tensor(a_lo[:, 2 + i, 0:SEQ], PS[:, b, 0:SEQ], col[:, C_PS + i:C_PS + i + 1],
                                         a_hi[:, 2 + i, 0:SEQ].bitcast(F32), ALU.mult, ALU.subtract).then_inc(aux_free, ax.up())
            for t in range(HEADS1):
                b = aux_bank()
                dve.scalar_tensor_tensor(qk[:, t, 0:SEQ], qk[:, t, 0:SEQ], col[:, C_SUB:C_SUB + 1], PS[:, b, 0:SEQ],
                                         ALU.mult, ALU.mult).then_inc(aux_free, ax.up())
            for t in range(HEADS1):
                dve.wait_ge(mix1_hi, 4 + t + 1)
                dve.wait_ge(aux_free, B1E["o_cast", t] + 1)
                dve.tensor_tensor(a_lo[:, 4 + t, 0:SEQ], qk[:, t, 0:SEQ], a_hi[:, 4 + t, 0:SEQ].bitcast(F32),
                                  ALU.subtract).then_inc(mix1_lo, 1)
            for c in range(OUT1):
                n = IN1 + c
                dve.wait_ge(chunk_used, n + 1)
                dve.scalar_tensor_tensor(h[:, c, 0:SEQ], PS[:, bank(n), 0:SEQ], 1.0, h[:, c, 0:SEQ],
                                         ALU.mult, ALU.add).then_inc(out_free, 1)
                dve.wait_ge(out_free, n + 1)
                gain = col[:, C_G + KD + c:C_G + KD + c + 1]
                step(dve.tensor_scalar(qk[:, 8 + c, 0:SEQ], h[:, c, 0:SEQ], gain, None, ALU.mult))
                split_lo(n + AHEAD, (n + AHEAD) % RING)
                norm_lo(1, c)
            split_lo(IN1 + OUT1 + AHEAD, (IN1 + OUT1 + AHEAD) % RING)
            mean_square(1)
            b = aux_bank()
            dve.tensor_tensor(S_f[0:20, 0:SEQ], PS[0:20, b, 0:SEQ], rstd[0:20, 0:SEQ], ALU.mult).then_inc(aux_free, ax.up())
            dve.wait_ge(aux_free, ax.now)
            dve.tensor_scalar(S_f[0:20, 0:SEQ], S_f[0:20, 0:SEQ], col[0:20, C_RB:C_RB + 1], None, ALU.add)\
               .then_inc(router_logits, 1)
            b = aux_bank()
            LG = S_f[:, 512:552]
            dve.tensor_copy(LG, PS[:, b, 0:40]).then_inc(aux_free, ax.up())
            dve.wait_ge(aux_free, ax.now)
            LG3 = LG.rearrange("p (t x) -> p t x", t=2)
            first_of = S_f[:, 640:644]
            for i in range(4):
                step(dve.memset(S_f[:, 640 + i:641 + i], float(4 - i)))

            def first_max(src, top, onehot):
                step(dve.tensor_reduce(top, src, AX.X, ALU.max))
                step(dve.tensor_tensor(onehot, src, top.unsqueeze(2).to_broadcast([P, 2, 4]), ALU.is_equal))
                step(dve.tensor_tensor(onehot, onehot, first_of.unsqueeze(1).to_broadcast([P, 2, 4]), ALU.mult))
                step(dve.tensor_reduce(S_f[:, 644:646], onehot, AX.X, ALU.max))
                step(dve.tensor_tensor(onehot, onehot, S_f[:, 644:646].unsqueeze(2).to_broadcast([P, 2, 4]), ALU.is_equal))

            def v24(off):
                return S_f[:, off:off + 8].rearrange("p (t x) -> p t x", t=2)

            mg, og, le, o1, o2 = S_f[:, 646:648], v24(648), v24(656), v24(664), v24(672)
            m1, m2, gp, den = S_f[:, 680:682], S_f[:, 682:684], S_f[:, 684:686], S_f[:, 686:688]
            grp = LG3[:, :, 0:4]
            first_max(grp, mg, og)
            dve.tensor_tensor(small_g().rearrange("p (t x) -> p t x", t=2), grp, mg.unsqueeze(2).to_broadcast([P, 2, 4]),
                              ALU.subtract).then_inc(router_centred, 1)
            t4 = S_f[:, 700:732].rearrange("p (t e g) -> p t e g", t=2, e=4)
            for t in range(2):
                step(dve.tensor_tensor(t4[:, t], LG3[:, t, 4:20].rearrange("p (g e) -> p e g", g=4),
                                       og[:, t].unsqueeze(1).to_broadcast([P, 4, 4]), ALU.mult))
            step(dve.tensor_reduce(le, t4, AX.X, ALU.add))
            first_max(le, m1, o1)
            t24 = v24(732)
            step(dve.scalar_tensor_tensor(t24, o1, -1.0e30, le, ALU.mult, ALU.add))
            first_max(t24, m2, o2)
            dve.tensor_tensor(small[:, 90:92], m2, m1, ALU.subtract).then_inc(router_centred, 1)
            dve.wait_ge(router_exp, 1)
            step(dve.tensor_reduce(gp, small_g().rearrange("p (t x) -> p t x", t=2), AX.X, ALU.add))
            dve.wait_ge(router_exp, 2)
            step(dve.tensor_scalar(den, small[:, 90:92], 1.0, None, ALU.add))
            step(dve.tensor_tensor(den, den, gp, ALU.mult))
            step(dve.reciprocal(den, den))
            step(dve.tensor_tensor(gp, den, small[:, 90:92], ALU.mult))
            step(dve.tensor_tensor(o1, o1, den.unsqueeze(2).to_broadcast([P, 2, 4]), ALU.mult))
            step(dve.tensor_tensor(o2, o2, gp.unsqueeze(2).to_broadcast([P, 2, 4]), ALU.mult))
            step(dve.tensor_tensor(o1, o1, o2, ALU.add))
            for t in range(2):
                gt = S_f[:, 600 + 16 * t:616 + 16 * t].rearrange("p (g e) -> p g e", g=4)
                dve.tensor_tensor(gt, o1[:, t].unsqueeze(1).to_broadcast([P, 4, 4]),
                                  og[:, t].unsqueeze(2).to_broadcast([P, 4, 4]), ALU.mult).then_inc(gates_ready, 1)
            b = aux_bank()
            dve.tensor_copy(gates_T, PS[0:16, b, 0:SEQ]).then_inc(aux_free, ax.up())

            def gates_cast(half):
                for e in range(4 * half, 4 * half + 4):
                    b = aux_bank()
                    dve.tensor_tensor(gates_bc[:, 2 * e:2 * e + 2, :], PS[:, b, 0:512].rearrange("p (u t) -> p u t", u=2),
                                      rstd[:, 0:SEQ].unsqueeze(1).to_broadcast([P, 2, SEQ]), ALU.mult).then_inc(aux_free, ax.up())
                dve.wait_ge(aux_free, ax.now)

            gates_cast(0)
            cb, ob = IN1 + OUT1, IN1 + OUT1
            for half in range(2):
                ffn_up(cb, cb % RING, ob, bank(ob), MOE_HALF, SEQ, None, half * 8, half == 0)
                down(cb + 2 * MOE_HALF, (cb + 2 * MOE_HALF) % RING, ob + 2 * MOE_HALF, bank(ob + 2 * MOE_HALF),
                     MOE_HALF, 1.0, 2 if half else None, SEQ, None if half else (lambda m: gates_cast(1) if m == 1 else None))
                cb += MOE_C
                ob += 2 * MOE_HALF + KD
            assert ax.n == B1_AUX
            dve.memset(biasB[:, :, :, SEQ:L], 0.0).then_inc(setup_done, 1)

            with dve.Fori(0, LAYERS) as l:
                ax.enter(l, LAYER_A)
                st.enter(l, DVE_STEPS)
                cb = l * LAYER_C + B1_CHUNKS
                ob = l * LAYER_O + B1_OUTS
                sl, bk = B2S, B2B
                ff.enter(l, 2 * FT)
                ffn_up(cb, sl, ob, bk, FT, L, l * 3 + 2)
                down(cb + FFN_UP, (sl + FFN_UP) % RING, ob + FFN_UP, (bk + FFN_UP) % 4, FT, 0.5, l * 3 + 3, L)
                c, o = FFN_C, FFN_UP + KD
                swaps = 0
                for t, (kind, i) in enumerate(QKV_ORDER):
                    split_lo(cb + (c + t + AHEAD), (sl + c + t + AHEAD) % RING)
                    if t == 0:
                        mean_square(l * 3 + 3)
                    dve.wait_ge(chunk_used, cb + (c + t + 1))
                    ps = PS[:, (bk + o + t) % 4, 0:L]
                    dst = vstage[i % 2] if kind == "v" else qk[:, R_OF[kind] + i, :]
                    if kind == "qB":
                        dve.scalar_tensor_tensor(dst, ps, 0.125, rstd[:, :], ALU.mult, ALU.mult).then_inc(out_free, 1)
                    else:
                        dve.tensor_tensor(dst, ps, rstd[:, :], ALU.mult).then_inc(out_free, 1)
                    for what, i in QKV_EVENTS.get(t, []):
                        if what == "stat":
                            continue
                        b = aux_bank()
                        if what in ("swapA", "swapC"):
                            tab = M_TAB + (0 if what == "swapA" else 2 * L)
                            if swaps >= 3:
                                dve.wait_ge(roped, l * 10 + swaps - 2)
                            dve.tensor_tensor(G[:, 17 + swaps % 3, :], PS[:, b, 0:L], mat[:, tab + L:tab + 2 * L], ALU.mult)\
                               .then_inc(aux_free, ax.up())
                            swaps += 1
                        elif what == "v":
                            step(dve.tensor_copy(v_tok[:, 0:2, i * P:(i + 1) * P],
                                                 PS[:, b, 0:2 * P].rearrange("p (k c) -> p k c", k=2)))
                            dve.tensor_copy(v_tok[0:META, 2, i * P:(i + 1) * P], PS[0:META, b, 2 * P:3 * P])\
                               .then_inc(aux_free, ax.up())
                        elif what == "sumC":
                            dve.tensor_scalar(G[0:10, 8, :], PS[0:10, b, 0:L], 1.0 / HD, EPS, ALU.mult, ALU.add)\
                               .then_inc(aux_free, ax.up())
                            inverse_root(G[0:10, 8, :], G[0:10, 9, :], c_rstd, 1)
                        else:
                            r = C_TILES[i]
                            gn = bass.ds(l * 2 + C_QN + (1 if i == 0 else 0), 1)
                            dve.scalar_tensor_tensor(qk[:, r, :], qk[:, r, :], col[:, gn], PS[:, b, 0:L],
                                                     ALU.mult, ALU.mult).then_inc(aux_free, ax.up())
                c, o = c + QKV_T, o + QKV_T
                nexp = Count()

                def turned(j):
                    dve.wait_ge(probsT_out, l * 24 + j + 1)
                    dve.tensor_copy(PT[:, 0, :], PS[:, 5, 0:L]).then_inc(probsT_dve, 1)
                    dve.tensor_copy(PT[0:META, 2, 0:P], PS[0:META, 5, L:L + P]).then_inc(probsT_dve, 1)
                    dve.tensor_copy(PT[0:META, 2, 2 * P:L], PS[0:META, 5, L + P:L + P + META]).then_inc(probsT_dve, 1)

                for j in range(24):
                    typ = j // 8
                    if j == 0:
                        step(dve.tensor_scalar(small[:, 68:76], col[:, bass.ds(l * 8 + C_SINK, 8)], -1.0, None, ALU.mult))
                    split_lo(cb + (c + j + AHEAD), (sl + c + j + AHEAD) % RING)
                    dve.wait_ge(scores_out, l * 72 + 3 * j + 3)
                    if typ == 1:
                        dve.wait_ge(bias_ready, l * 8 + (j - 8 + 1))
                    dve.tensor_copy(small[0:1, 94:95], small[0:1, 93:94])
                    jj = 3 * (j % 2)
                    for qt in range(3):
                        r = q_rows(qt)
                        if typ == 0:
                            bias = mat[0:r, M_MA + qt * L:M_MA + (qt + 1) * L]
                            hA = j // 2 + 4 * (j % 2)
                            init = small[0:r, 68 + hA:69 + hA]
                        elif typ == 1:
                            bias = biasB[:, j % 2, qt, :] if qt < 2 else mat[0:r, M_MBM:M_MBM + L]
                            init = 3.0e38
                        else:
                            bias = zero[0:r, :].to_broadcast([r, L])
                            init = 3.0e38
                        dve.tensor_tensor_reduce(S_sb[0:r, j % 2, qt, :], PS[0:r, 2 + qt, 0:L], bias,
                                                 -1.0 if typ == 1 else -0.125, init, ALU.add, ALU.min,
                                                 minl[0:r, jj + qt:jj + qt + 1]).then_inc(logits_ready, 1)
                    if j % 2 == 1 and j > 1:
                        pair_lo(dve, l, (j - 3) // 2)
                    if j > 0:
                        turned(j - 1)
                    nexp.up(4 if j < 8 else 3)
                    dve.wait_ge(exp_done, l * 80 + nexp.n)
                    total = rsum
                    if j < 8:
                        total = esink
                        step(dve.tensor_tensor(esink[:, jj:jj + 3], rsum[:, jj:jj + 3], esink[:, jj:jj + 3], ALU.add))
                    dve.reciprocal(rden[:, jj:jj + 3], total[:, jj:jj + 3]).then_inc(rden_ready, 1)
                    dve.wait_ge(chunk_used, cb + (c + j + 1))
                    dve.tensor_tensor(G[:, j, :], PS[:, j % 2, 0:L], rstd[:, :], ALU.mult).then_inc(out_free, 1)
                turned(23)
                pair_lo(dve, l, 11)
                c, o = c + GATE_T, o + GATE_T

                def mixed_lo(m):
                    dve.wait_ge(mix_hi_done, l * KD + m + 1)
                    dve.tensor_tensor(a_lo[:, 12 + m, :], S_sb[:, m % 2, 0, :], a_hi[:, 12 + m, :].bitcast(F32),
                                      ALU.subtract).then_inc(mix_lo_done, 1)

                for s in range(BRANCH_C):
                    split_lo(cb + (c + s + AHEAD), (sl + c + s + AHEAD) % RING)
                    dve.wait_ge(chunk_used, cb + (c + s + 1))
                    for u in (2 * s, 2 * s + 1):
                        n, m = u % 3, u // 3
                        dve.wait_ge(gate_sig, l * 24 + u + 1)
                        if n == 0 and m >= 2:
                            dve.wait_ge(mix_lo_done, l * KD + m - 1)
                        dve.tensor_tensor(S_sb[:, m % 2, n, :], PS[:, (bk + o + u) % 4, 0:L], G[:, n * KD + m, :],
                                          ALU.mult).then_inc(out_free, 1)
                        if n == 2 and m > 0:
                            mixed_lo(m - 1)
                mixed_lo(KD - 1)
                c, o = c + BRANCH_C, o + 3 * KD
                for m in range(OUT_C):
                    dve.wait_ge(chunk_used, cb + (c + m + 1))
                    residual(None, m, ob + (o + m), (bk + o + m) % 4, 1.0, L)
                    split_lo(cb + (c + m + AHEAD), (sl + c + m + AHEAD) % RING)
                    norm_lo(l * 3 + 4, m)
                c, o = c + OUT_C, o + KD
                ffn_up(cb + c, (sl + c) % RING, ob + o, (bk + o) % 4, FT, L, l * 3 + 4)
                down(cb + (c + FFN_UP), (sl + c + FFN_UP) % RING, ob + (o + FFN_UP), (bk + o + FFN_UP) % 4, FT, 0.5, l * 3 + 5, L)
                ff.leave(LAYERS)
                st.leave(LAYERS)
                ax.leave(LAYERS)
            mean_square(8)
            for m in range(KD):
                dve.scalar_tensor_tensor(qk[:, m, 0:SEQ], h[:, m, 0:SEQ], col[:, C_G + 8 * KD + m:C_G + 8 * KD + m + 1],
                                         rstd[:, 0:SEQ], ALU.mult, ALU.mult).then_inc(out_ready, 1)

        @block.gpsimd
        def _(pool):
            st = Count()

            def step(ins):
                ins.then_inc(pool_step, st.up())
                pool.wait_ge(pool_step, st.now)

            def sum_squares(o, n=KD):
                for m in range(n):
                    if o is not None:
                        pool.wait_ge(out_free, o + (m + 1))
                    if m == 0:
                        step(pool.tensor_tensor(acc, h[:, 0, :], h[:, 0, :], ALU.mult))
                        continue
                    step(pool.tensor_tensor(sq, h[:, m, :], h[:, m, :], ALU.mult))
                    ins = pool.tensor_tensor(acc, acc, sq, ALU.add)
                    if m < n - 1:
                        step(ins)
                    else:
                        ins.then_inc(squares_summed, 1)

            pool.wait_ge(setup_done, 1)
            pool.wait_ge(inputs_landed, 32)
            sum_squares(None, KD // 2)
            pool.wait_ge(out_free, 2)
            for i in range(2):
                pool.wait_ge(conv_gate, i + 1)
                pool.tensor_tensor(U[:, i, CONVW - 1:], qk[:, i, 0:SEQ], qk[:, 2 + i, 0:SEQ], ALU.mult).then_inc(conv_input, 1)
            pool.wait_ge(conv_input, 2)
            pool.dma_start(spread_sb, spread).then_inc(spread_landed, 16)
            w = col[:, C_CONVW + 1:C_CONVW + 2]
            pool.tensor_scalar(Y[:, 1, :], U[:, 1, 0:SEQ], w, col[:, C_CONVB + 1:C_CONVB + 2], ALU.mult, ALU.add)\
                .then_inc(tap_added, 1)
            for k in range(1, CONVW):
                pool.wait_ge(tap_product, k)
                pool.wait_ge(tap_added, k)
                pool.tensor_tensor(Y[:, 1, :], Y[:, 1, :], tap_products[k % 3][:, 0:SEQ], ALU.add)\
                    .then_inc(tap_added if k < CONVW - 1 else conv1_done, 1)
            pool.wait_ge(out_free, 6)
            pool.wait_ge(consts_landed, ALL_CONSTS)
            step(pool.tensor_copy(UP[:, :, 16:272], qk[:, 4:6, 0:SEQ]))
            ladder = [UW, S_f[:, 1024:1568].rearrange("p (i t) -> p i t", i=2)]
            last, w = UP, 1
            for g in range(4):
                nxt, r0 = ladder[g % 2], 2 * w - 1
                step(pool.tensor_tensor(nxt[:, :, r0:272], last[:, :, r0:272], last[:, :, r0 - w:272 - w], ALU.add))
                t, p0 = g // 2, 64 * (g % 2)
                step(pool.tensor_tensor(qk[p0:p0 + 64, 4 + t, 0:SEQ], nxt[p0:p0 + 64, t, 16:272],
                                        invcount[p0:p0 + 64, t, :], ALU.mult))
                last, w = nxt, 2 * w
            pool.tensor_tensor(qk[:, 4:6, 0:SEQ], qk[:, 4:6, 0:SEQ], UP[:, :, 16:272], ALU.subtract).then_inc(pooled, 1)
            sum_squares(IN1)
            sum_squares(B1_OUTS - KD)

            with pool.Fori(0, LAYERS) as l:
                st.enter(l, POOL_STEPS)
                ob = l * LAYER_O + B1_OUTS
                sum_squares(ob + FFN_UP)
                SWAPS = [(k, e) for k, e in enumerate(QKV_EVENT_LIST) if e[0] in ("swapA", "swapC")]
                for n, (k, (what, i)) in enumerate(SWAPS):
                    tab = M_TAB + (0 if what == "swapA" else 2 * L)
                    pool.wait_ge(aux_free, l * LAYER_A + (B1_AUX + 1 + k + 1))
                    step(pool.tensor_tensor(qk[:, i, :], qk[:, i, :], mat[:, tab:tab + L], ALU.mult))
                    pool.tensor_tensor(qk[:, i, :], qk[:, i, :], G[:, 17 + n % 3, :], ALU.add).then_inc(roped, 1)
                for j in range(24):
                    pool.wait_ge(rden_ready, l * 24 + j + 1)
                    for qt in range(3):
                        r = q_rows(qt)
                        e = 3 * (j % 2) + qt
                        pool.tensor_tensor(S_sb[0:r, j % 2, qt, :], S_sb[0:r, j % 2, qt, :],
                                           rden[0:r, e:e + 1].to_broadcast([r, L]), ALU.mult).then_inc(probs_ready, 1)
                    if 7 <= j < 15:
                        hB = j - 7
                        pool.wait_ge(bias_landed[hB % 2], l * 256 + 64 * (hB // 2 + 1))
                        for qt in range(2):
                            ins = pool.tensor_tensor(biasB[:, hB % 2, qt, 0:SEQ], biasB[:, hB % 2, qt, 0:SEQ],
                                                     mat[:, M_MB + qt * SEQ:M_MB + (qt + 1) * SEQ], ALU.add)
                            if qt == 0:
                                step(ins)
                            else:
                                ins.then_inc(bias_ready, 1)
                ro = ob + (FFN_UP + KD + QKV_T + GATE_T)
                for m in range(KD):
                    total = S_sb[:, m % 2, 0, :]
                    for n in (1, 2):
                        pool.wait_ge(out_free, ro + (3 * m + n + 1))
                        ins = pool.tensor_tensor(total, total, S_sb[:, m % 2, n, :], ALU.add)
                        if n == 1:
                            step(ins)
                        else:
                            ins.then_inc(mixed_ready, 1)
                sum_squares(ob + (FFN_UP + KD + QKV_T + GATE_T + 3 * KD))
                sum_squares(ob + (LAYER_O - KD))
                st.leave(LAYERS)


def dense_mask(allowed):
    return np.where(allowed, 0.0, -1.0e30).astype(np.float32)


def by_query_tile(a):
    n = -(-a.shape[0] // P)
    full = np.zeros((n * P, a.shape[1]), np.float32)
    full[:a.shape[0]] = a
    return full.reshape(n, P, -1).transpose(1, 0, 2).reshape(P, -1)


def constants():
    c = np.zeros((P, NM), np.float32)
    c[:, M_ID:M_ID + P] = np.eye(P)
    c[:, M_ONES:M_ONES + P] = 1.0
    p = np.arange(P)
    c[(p + 32) % 64 + p // 64 * 64, M_PA + p] = 1.0
    c[(p + 16) % 32 + p // 32 * 32, M_PC + p] = 1.0
    for t in range(8):
        c[p, M_SEL16 + 17 * t + 2 * t + p // 64] = 1.0
    c[:, M_SEL16 + 17 * 8 + 16] = HD / 256
    for t in range(4):
        c[:, M_SEL4 + 4 * t + t] = 1.0
    pos = np.concatenate([np.arange(SEQ) + META, np.arange(META)])
    t = pos - META
    row = np.where(t >= 0, t // 64, -1).astype(np.float32)
    column = np.where(t >= 0, t % 64, pos).astype(np.float32)

    def table(dim, where):
        inv = np.float32(10000.0) ** (-np.arange(0, dim, 2, dtype=np.float32) / np.float32(dim))
        ang = (where.astype(np.float32)[None, :] * inv[:, None]).astype(np.float32)
        cos, sin = np.cos(ang), np.sin(ang)
        return np.concatenate([cos, cos]), np.concatenate([-sin, sin])

    cosA, sinA = table(64, pos)
    (cr, sr), (cc, sc) = table(32, row), table(32, column)
    for k, a in enumerate((cosA, sinA, np.concatenate([cr, cc]), np.concatenate([sr, sc]))):
        c[:, M_TAB + k * L:M_TAB + (k + 1) * L] = np.concatenate([a, a])
    real = t >= 0
    band = (np.abs(pos[:, None] - pos[None, :]) <= 128) | ~real[None, :]
    c[:, M_MA:M_MA + 3 * L] = by_query_tile(dense_mask(band))
    c[:META, M_MBM:M_MBM + L] = dense_mask(np.broadcast_to(~real[None, :], (META, L)))
    qc = np.arange(SEQ) % 64
    start = np.clip(qc - 8, 0, 64 - 16)
    kc = qc[None, :]
    ok = (kc >= start[:, None]) & (kc < start[:, None] + 16)
    c[:, M_MB:M_MB + 2 * SEQ] = by_query_tile(dense_mask(ok))
    return c


def block1_constants():
    c = np.zeros((P, 2048 + 512), np.float32)
    tq = np.arange(SEQ)
    dist = (tq[:, None] - tq[None, :]).astype(np.float32)
    start = 2.0 ** (-8.0 / HEADS1)
    for hd in range(HEADS1):
        bias = np.where(dist >= 0, -np.float32(start ** (hd + 1)) * dist * 8, -1.0e30)
        c[:, hd * 512:(hd + 1) * 512] = by_query_tile(bias)
    for g, win in enumerate((2, 4, 8, 16)):
        inv = 1.0 / np.minimum(tq + 1, win).astype(np.float32)
        c[64 * (g % 2):64 * (g % 2) + 64, 2048 + SEQ * (g // 2):2048 + SEQ * (g // 2 + 1)] = inv
    return c


def spread_constants():
    c = np.zeros((16, 8 * P), np.float32)
    for r in range(16):
        c[r, 64 * r:64 * r + 64] = 1.0
    return c


def tiles(w):
    K, N = w.shape
    return w.reshape(K // P, P, N // P, P).transpose(2, 0, 1, 3)


def kernel(**inputs):
    import concourse.bacc as bacc
    from concourse.bass_utils import run_bass_kernel_spmd

    a = {k: np.asarray(v) for k, v in inputs.items()}
    f = np.float32

    stream = np.empty((STREAM, P, BLK, P), f)
    at = 0

    def put(blocks):
        nonlocal at
        n = blocks.shape[0] // BLK
        stream[at:at + n] = blocks.reshape(n, BLK, P, P).transpose(0, 2, 1, 3)
        at += n

    def put_w(w):
        put(tiles(w).reshape(-1, P, P))

    w = a["w_in"][0]
    put_w(w)
    put_w(a["w_out"][0])
    for half in range(2):
        es = range(8 * half, 8 * half + 8)
        for e in es:
            g, u = tiles(a["w_gate"][0, e]), tiles(a["w_up"][0, e])
            put(np.stack([g, u], 1).reshape(-1, P, P))
        put_w(a["w_down"][0, 8 * half:8 * half + 8].reshape(-1, D))

    def ffn(w_in, w_out):
        g, u = tiles(w_in[:, :FF]), tiles(w_in[:, FF:])
        put(np.stack([g, u], 1).reshape(-1, P, P))
        put_w(w_out)

    pairs = np.concatenate([np.r_[64 * t:64 * t + 64, 64 * (t + 4):64 * (t + 4) + 64] for t in range(4)])
    for l in range(LAYERS):
        ffn(a["ffn1_w_in_2"][l], a["ffn1_w_out_2"][l])
        w = a["w_in_2"][l]
        qa, ka, va, qb, kb, vb, qc, kc, vc, gates = np.split(w, np.cumsum([512, 128, 128, 512, 512, 512, 512, 128, 128]), axis=1)
        for part in (ka, kc, kb, va, vc, vb, qc[:, pairs], qa[:, pairs], qb, gates):
            put_w(part)
        wb = [a["w_branch_2"][l, 0][pairs], a["w_branch_2"][l, 1], a["w_branch_2"][l, 2][pairs]]
        put(np.stack([tiles(x) for x in wb], 1).reshape(-1, P, P))
        put_w(a["w_out_2"][l])
        ffn(a["ffn2_w_in_2"][l], a["ffn2_w_out_2"][l])
    assert at == CHUNKS
    stream[at:] = stream[:STREAM - at]

    col = np.zeros((P, NC), f)

    def by_tile(v):
        return v.reshape(-1, P).T

    gains = [a["attn_norm_g"][0], a["ffn_norm_g"][0]]
    for l in range(LAYERS):
        gains += [a["ffn1_norm_2"][l], a["mix_norm_2"][l], a["ffn2_norm_2"][l]]
    gains.append(a["final_norm_2"])
    for v, g in enumerate(gains):
        col[:, C_G + v * KD:C_G + (v + 1) * KD] = by_tile(g)
    for l in range(LAYERS):
        col[:, C_QN + 2 * l] = np.tile(a["qnorm_c_2"][l], 2)
        col[:, C_QN + 2 * l + 1] = np.tile(a["knorm_c_2"][l], 2)
        col[:, C_SINK + 8 * l:C_SINK + 8 * l + 8] = a["sink_a_2"][l][None, :]
    for k in range(CONVW):
        col[:, C_CONVW + 2 * k:C_CONVW + 2 * k + 2] = by_tile(a["conv_w"][0, k])
    for at_, name in ((C_CONVB, "conv_b"), (C_LNG, "conv_ln_g"), (C_LNB, "conv_ln_b"), (C_PWB, "conv_pw_b"), (C_PS, "pool_scale")):
        col[:, at_:at_ + 2] = by_tile(a[name][0])
    col[:, C_QN1] = np.tile(a["q_norm_g"][0], 2)
    col[:, C_QN1 + 1] = np.tile(a["k_norm_g"][0], 2)
    col[:, C_SUB] = a["attn_sub_norm_g"][0]
    for k, name in enumerate(("lambda_q1", "lambda_k1", "lambda_q2", "lambda_k2")):
        col[:64, C_LAM + k] = a[name][0]
    col[:20, C_RB] = np.concatenate([a["router_g_b"][0], a["router_e_b"][0]])
    rw = np.concatenate([a["router_g_w"][0], a["router_e_w"][0]], axis=1)
    col[:, C_RW:] = rw.reshape(KD, P, 20).transpose(1, 0, 2).reshape(P, -1)

    b1 = np.zeros((P, 2048 + 512 + 512 + 256), f)
    b1[:, :2560] = block1_constants()
    b1[:, 2560:3072] = a["conv_pw_w"][0].reshape(2, P, 256).transpose(1, 0, 2).reshape(P, -1)
    for g in range(4):
        p0 = 64 * (g % 2)
        b1[p0:p0 + 64, 3072 + P * (g // 2) + p0:3072 + P * (g // 2) + p0 + 64] = a["pool_w"][0, g]

    rpb = np.zeros((LAYERS, 8, 7, 64, 128), f)
    rpb[:, :, :, :, 48:79] = a["rpb_b_2"][:, :, 4:11, None, :]

    x = np.concatenate([a["x"][0], a["meta_tokens_2"]], axis=0)
    xT = x.T.reshape(KD, P, L).transpose(1, 0, 2)

    arrays = {
        "stream": stream.reshape(STREAM, P, BLK * P), "xT": xT, "cols": col, "mats": constants(), "b1mats": b1,
        "spread": spread_constants(),
        "rpbz": rpb,
    }
    arrays = {k: np.ascontiguousarray(v) for k, v in arrays.items()}
    nc = bacc.Bacc("TRN2", target_bir_lowering=False, num_devices=1)
    args = [nc.dram_tensor(k, v.shape, F32, kind="ExternalInput").ap() for k, v in arrays.items()]
    out = nc.dram_tensor("out", (P, KD, SEQ), F32, kind="ExternalOutput").ap()
    build(nc, *args, out)
    got = run_bass_kernel_spmd(nc, [arrays], core_ids=[0]).results[0]["out"]
    return np.ascontiguousarray(got.transpose(2, 1, 0).reshape(1, SEQ, D))
```
